# Optimizing a Trainium2 kernel written in Bass

```python
import math
import jax
import jax.numpy as jnp
from jax import lax
import numpy as np
import jax, jax.numpy as jnp

D_MODEL = 1024
BATCH = 1
SEQ = 512
DEPTH = 1

MIX_WIDTH = D_MODEL
HEAD_DIM = 64
ATT_WIDTH = MIX_WIDTH // 2
ATT_HEADS = ATT_WIDTH // HEAD_DIM
IDX_HEADS = 4
IDX_DIM = HEAD_DIM
TOPK_MAX = 256
Q_BLOCK = 128
ROPE_THETA = 10000.0
INDEXER_SCALE = (IDX_HEADS ** -0.5) * (IDX_DIM ** -0.5)
SSD_WIDTH = MIX_WIDTH - ATT_WIDTH
SSD_HEAD_DIM = 64
SSD_HEADS = SSD_WIDTH // SSD_HEAD_DIM
SSD_GROUPS = 2
D_STATE = 64
CONV_WIDTH = 4
CONV_CH = SSD_WIDTH + 2 * SSD_GROUPS * D_STATE
CHUNK = 128
N_GROUPS_MOE = 4
EXPERTS_PER_GROUP = 4
N_EXPERTS = N_GROUPS_MOE * EXPERTS_PER_GROUP
TOP_K_IN_GROUP = 2
EXPERT_FF = 256
ALPHA = (2 * DEPTH) ** 0.25
BETA = (8 * DEPTH) ** -0.25
LN_EPS = 1e-5
IN_SPLIT_SIZES = (ATT_WIDTH, HEAD_DIM, HEAD_DIM, IDX_HEADS * IDX_DIM, IDX_DIM, IDX_HEADS, SSD_WIDTH, CONV_CH, SSD_HEADS)
IN_WIDTH = sum(IN_SPLIT_SIZES)
IN_SPLIT_POINTS = tuple(int(v) for v in np.cumsum(IN_SPLIT_SIZES)[:-1])


def layer_norm(x, g, b):
    xf = x.astype(jnp.float32)
    mu = jnp.mean(xf, -1, keepdims=True)
    var = jnp.mean(jnp.square(xf - mu), -1, keepdims=True)
    return ((xf - mu) * lax.rsqrt(var + LN_EPS)).astype(x.dtype) * g + b

def rope_tables(seq_len):
    inv = ROPE_THETA ** (-jnp.arange(0, HEAD_DIM, 2, dtype=jnp.float32) / HEAD_DIM)
    ang = jnp.arange(seq_len, dtype=jnp.float32)[:, None] * inv[None, :]
    return jnp.cos(ang), jnp.sin(ang)

def apply_rope(x, cos, sin):
    half = x.shape[-1] // 2
    x1, x2 = x[..., :half], x[..., half:]
    cos = cos.astype(x.dtype)
    sin = sin.astype(x.dtype)
    return jnp.concatenate([x1 * cos - x2 * sin, x1 * sin + x2 * cos], -1)

def dsa_attention(q, k, v, iq, ik, iw, topk):
    bsz, s, h, dh = q.shape
    n_blocks = s // Q_BLOCK
    key_pos = jnp.arange(s)

    def block(i):
        t0 = i * Q_BLOCK
        qb = lax.dynamic_slice_in_dim(q, t0, Q_BLOCK, 1)
        iqb = lax.dynamic_slice_in_dim(iq, t0, Q_BLOCK, 1)
        iwb = lax.dynamic_slice_in_dim(iw, t0, Q_BLOCK, 1)
        qpos = t0 + jnp.arange(Q_BLOCK)
        causal = key_pos[None, :] <= qpos[:, None]
        sc = jax.nn.relu(jnp.einsum('bthd,bsd->bths', iqb, ik))
        sc = jnp.einsum('bths,bth->bts', sc, iwb).astype(jnp.float32)
        sc = jnp.where(causal[None], sc, -jnp.inf)
        _, sel = lax.top_k(sc, topk)
        valid = sel <= qpos[None, :, None]
        k_sel = jax.vmap(lambda a, idx: a[idx])(k, sel)
        v_sel = jax.vmap(lambda a, idx: a[idx])(v, sel)
        logits = jnp.einsum('bthd,btkd->bthk', qb, k_sel).astype(jnp.float32) * (dh ** -0.5)
        logits = jnp.where(valid[:, :, None, :], logits, -jnp.inf)
        p = jax.nn.softmax(logits, -1).astype(v.dtype)
        return jnp.einsum('bthk,btkd->bthd', p, v_sel)

    out = lax.map(block, jnp.arange(n_blocks))
    return jnp.moveaxis(out, 0, 1).reshape(bsz, s, h * dh)

def causal_depthwise_conv(u, w, b):
    out = lax.conv_general_dilated(
        u, w[:, None, :].astype(u.dtype), window_strides=(1,),
        padding=[(CONV_WIDTH - 1, 0)], dimension_numbers=('NWC', 'WIO', 'NWC'),
        feature_group_count=u.shape[-1])
    return out + b

def segsum(a):
    t = a.shape[-1]
    ar = jnp.broadcast_to(a[..., :, None], a.shape + (t,))
    strict = jnp.tril(jnp.ones((t, t), dtype=bool), -1)
    cs = jnp.cumsum(jnp.where(strict, ar, 0.0), axis=-2)
    return jnp.where(jnp.tril(jnp.ones((t, t), dtype=bool)), cs, -jnp.inf)

def ssd_chunked(xdt, adt, bm, cm):
    b, s, h, p = xdt.shape
    n = bm.shape[-1]
    c = s // CHUNK
    X = xdt.reshape(b, c, CHUNK, h, p)
    Bc = bm.reshape(b, c, CHUNK, h, n)
    Cc = cm.reshape(b, c, CHUNK, h, n)
    A = adt.reshape(b, c, CHUNK, h).transpose(0, 3, 1, 2)
    a_cum = jnp.cumsum(A, -1)
    Lmat = jnp.exp(segsum(A))
    y_diag = jnp.einsum('bclhn,bcshn,bhcls,bcshp->bclhp', Cc, Bc, Lmat, X)
    decay_states = jnp.exp(a_cum[..., -1:] - a_cum)
    chunk_states = jnp.einsum('bclhn,bhcl,bclhp->bchpn', Bc, decay_states, X)
    chunk_decay = jnp.exp(a_cum[..., -1])

    def step(carry, inp):
        st, dec = inp
        return carry * dec[..., None, None] + st, carry

    init = jnp.zeros((b, h, p, n), X.dtype)
    _, prev = lax.scan(step, init, (jnp.moveaxis(chunk_states, 1, 0), jnp.moveaxis(chunk_decay, 2, 0)))
    prev = jnp.moveaxis(prev, 0, 1)
    y_off = jnp.einsum('bclhn,bchpn,bhcl->bclhp', Cc, prev, jnp.exp(a_cum))
    return (y_diag + y_off).reshape(b, s, h, p)

def ssd_mixer(z, xbc, dt_raw, conv_w, conv_b, dt_bias, a_log, d_skip, norm_w):
    bsz, s, _ = xbc.shape
    f32 = jnp.float32
    xbc = jax.nn.silu(causal_depthwise_conv(xbc, conv_w, conv_b))
    gn = SSD_GROUPS * D_STATE
    xs = xbc[..., :SSD_WIDTH].reshape(bsz, s, SSD_HEADS, SSD_HEAD_DIM).astype(f32)
    bm = xbc[..., SSD_WIDTH:SSD_WIDTH + gn].reshape(bsz, s, SSD_GROUPS, D_STATE)
    cm = xbc[..., SSD_WIDTH + gn:].reshape(bsz, s, SSD_GROUPS, D_STATE)
    rep = SSD_HEADS // SSD_GROUPS
    bm = jnp.repeat(bm, rep, axis=2).astype(f32)
    cm = jnp.repeat(cm, rep, axis=2).astype(f32)
    dt = jax.nn.softplus(dt_raw.astype(f32) + dt_bias.astype(f32))
    a = -jnp.exp(a_log.astype(f32))
    y = ssd_chunked(xs * dt[..., None], dt * a, bm, cm)
    y = y + d_skip.astype(f32)[:, None] * xs
    y = y.reshape(bsz, s, SSD_WIDTH) * jax.nn.silu(z.astype(f32))
    y = y * lax.rsqrt(jnp.mean(jnp.square(y), -1, keepdims=True) + LN_EPS)
    return y.astype(z.dtype) * norm_w

def hier_moe(h, w_rg, b_rg, w_re, b_re, w_gate, w_up, w_down):
    bsz, s, _ = h.shape
    f32 = jnp.float32
    p_group = jax.nn.softmax((h @ w_rg + b_rg).astype(f32), -1)
    g_idx = jnp.argmax(p_group, -1)
    g_prob = jnp.max(p_group, -1)
    e_logits = (h @ w_re + b_re).astype(f32).reshape(bsz, s, N_GROUPS_MOE, EXPERTS_PER_GROUP)
    e_in_group = jnp.take_along_axis(e_logits, g_idx[..., None, None], axis=2)[..., 0, :]
    top_logits, top_idx = lax.top_k(e_in_group, TOP_K_IN_GROUP)
    top_w = jax.nn.softmax(top_logits, -1) * g_prob[..., None]
    expert_id = g_idx[..., None] * EXPERTS_PER_GROUP + top_idx
    gates = jnp.sum(jax.nn.one_hot(expert_id, N_EXPERTS, dtype=f32) * top_w[..., None], axis=-2).astype(h.dtype)
    y = jnp.zeros_like(h)
    for e in range(N_EXPERTS):
        hid = jax.nn.silu(h @ w_gate[e]) * (h @ w_up[e])
        y = y + gates[..., e:e + 1] * (hid @ w_down[e])
    return y

def first_inputs(seed: int = 0) -> dict:
    key = jax.random.key(seed)
    ks = jax.random.split(key, 21)
    f32 = jnp.float32

    def nrm(k, shape, scale):
        return jax.random.normal(k, shape, f32) * scale

    x = nrm(ks[0], (BATCH, SEQ, D_MODEL), 1.0)
    w_in = nrm(ks[1], (DEPTH, D_MODEL, IN_WIDTH), D_MODEL ** -0.5)
    conv_w = nrm(ks[2], (DEPTH, CONV_WIDTH, CONV_CH), CONV_WIDTH ** -0.5)
    conv_b = nrm(ks[3], (DEPTH, CONV_CH), 0.02)
    dt0 = jnp.exp(jax.random.uniform(ks[4], (DEPTH, SSD_HEADS), f32, math.log(1e-3), math.log(1e-1)))
    dt_bias = dt0 + jnp.log(-jnp.expm1(-dt0))
    a_log = jnp.log(jax.random.uniform(ks[5], (DEPTH, SSD_HEADS), f32, 1.0, 16.0))
    d_skip = 1.0 + nrm(ks[6], (DEPTH, SSD_HEADS), 0.1)
    ssd_norm_w = 1.0 + nrm(ks[7], (DEPTH, SSD_WIDTH), 0.05)
    w_out = nrm(ks[8], (DEPTH, MIX_WIDTH, D_MODEL), (MIX_WIDTH ** -0.5) * BETA)
    ln1_g = 1.0 + nrm(ks[9], (DEPTH, D_MODEL), 0.05)
    ln1_b = nrm(ks[10], (DEPTH, D_MODEL), 0.02)
    w_route_group = nrm(ks[11], (DEPTH, D_MODEL, N_GROUPS_MOE), D_MODEL ** -0.5)
    b_route_group = nrm(ks[12], (DEPTH, N_GROUPS_MOE), 0.01)
    w_route_expert = nrm(ks[13], (DEPTH, D_MODEL, N_EXPERTS), D_MODEL ** -0.5)
    b_route_expert = nrm(ks[14], (DEPTH, N_EXPERTS), 0.01)
    w_gate = nrm(ks[15], (DEPTH, N_EXPERTS, D_MODEL, EXPERT_FF), D_MODEL ** -0.5)
    w_up = nrm(ks[16], (DEPTH, N_EXPERTS, D_MODEL, EXPERT_FF), D_MODEL ** -0.5)
    w_down = nrm(ks[17], (DEPTH, N_EXPERTS, EXPERT_FF, D_MODEL), (EXPERT_FF ** -0.5) * BETA)
    ln2_g = 1.0 + nrm(ks[18], (DEPTH, D_MODEL), 0.05)
    ln2_b = nrm(ks[19], (DEPTH, D_MODEL), 0.02)
    return {'x': x, 'w_in': w_in, 'conv_w': conv_w, 'conv_b': conv_b, 'dt_bias': dt_bias,
            'a_log': a_log, 'd_skip': d_skip, 'ssd_norm_w': ssd_norm_w, 'w_out': w_out,
            'ln1_g': ln1_g, 'ln1_b': ln1_b, 'w_route_group': w_route_group,
            'b_route_group': b_route_group, 'w_route_expert': w_route_expert,
            'b_route_expert': b_route_expert, 'w_gate': w_gate, 'w_up': w_up,
            'w_down': w_down, 'ln2_g': ln2_g, 'ln2_b': ln2_b}

def first_block(x, w_in, conv_w, conv_b, dt_bias, a_log, d_skip, ssd_norm_w, w_out, ln1_g, ln1_b,
              w_route_group, b_route_group, w_route_expert, b_route_expert, w_gate, w_up,
              w_down, ln2_g, ln2_b):
    bsz, s, _ = x.shape
    topk = min(TOPK_MAX, s // 4)
    cos, sin = rope_tables(s)
    cos_h, sin_h = cos[:, None, :], sin[:, None, :]
    for l in range(DEPTH):
        proj = jnp.einsum('bsd,de->bse', x, w_in[l])
        q, k, v, iq, ik, iw, z, xbc, dt_raw = jnp.split(proj, IN_SPLIT_POINTS, axis=-1)
        q = apply_rope(q.reshape(bsz, s, ATT_HEADS, HEAD_DIM), cos_h, sin_h)
        k = apply_rope(k, cos, sin)
        iq = apply_rope(iq.reshape(bsz, s, IDX_HEADS, IDX_DIM), cos_h, sin_h)
        ik = apply_rope(ik, cos, sin)
        att = dsa_attention(q, k, v, iq, ik, iw * INDEXER_SCALE, topk)
        ssd = ssd_mixer(z, xbc, dt_raw, conv_w[l], conv_b[l], dt_bias[l], a_log[l],
                        d_skip[l], ssd_norm_w[l])
        mixed = jnp.einsum('bse,ed->bsd', jnp.concatenate([att, ssd], -1), w_out[l])
        x = layer_norm(ALPHA * x + mixed, ln1_g[l], ln1_b[l])
        ffn = hier_moe(x, w_route_group[l], b_route_group[l], w_route_expert[l],
                       b_route_expert[l], w_gate[l], w_up[l], w_down[l])
        x = layer_norm(ALPHA * x + ffn, ln2_g[l], ln2_b[l])
    return x


DEPTH_2 = 2

MEM_LEN = 256
RNN_WIDTH = D_MODEL
RNN_BLOCKS = 4
RNN_BLOCK = RNN_WIDTH // RNN_BLOCKS
LRU_C = 8.0
N_Q_HEADS = D_MODEL // HEAD_DIM
N_KV_HEADS = 2
GROUP = N_Q_HEADS // N_KV_HEADS
ATTN_WIDTH = N_Q_HEADS * HEAD_DIM
KV_WIDTH = N_KV_HEADS * HEAD_DIM
WINDOW = 128
BLOCK = 128
ROPE_THETA_2 = 500000.0
ROT_DIM = HEAD_DIM // 4
IN_COLS = 2 * RNN_WIDTH + ATTN_WIDTH + 2 * KV_WIDTH + 2 * D_MODEL
CROSS_HEADS = 4
CROSS_HEAD_DIM = D_MODEL // CROSS_HEADS
CROSS_WIDTH = CROSS_HEADS * CROSS_HEAD_DIM
D_FF = -(-8 * D_MODEL // (3 * 256)) * 256
DEEPNORM_ALPHA = (2 * DEPTH_2) ** 0.25
DEEPNORM_BETA = (8 * DEPTH_2) ** -0.25
NEG_INF = -1e30


def layer_norm_2(x, g, b):
    xf = x.astype(jnp.float32)
    mu = jnp.mean(xf, axis=-1, keepdims=True)
    var = jnp.mean(jnp.square(xf - mu), axis=-1, keepdims=True)
    y = (xf - mu) * lax.rsqrt(var + LN_EPS)
    return (y * g.astype(jnp.float32) + b.astype(jnp.float32)).astype(x.dtype)

def rope_tables_2(seq_len):
    pos = jnp.arange(seq_len, dtype=jnp.float32)
    inv_freq = ROPE_THETA_2 ** (-jnp.arange(0, ROT_DIM, 2, dtype=jnp.float32) / ROT_DIM)
    ang = pos[:, None] * inv_freq[None, :]
    return jnp.cos(ang), jnp.sin(ang)

def apply_partial_rope(t, cos, sin):
    half = ROT_DIM // 2
    c = cos[None, :, None, :].astype(t.dtype)
    s = sin[None, :, None, :].astype(t.dtype)
    t1, t2, rest = t[..., :half], t[..., half:ROT_DIM], t[..., ROT_DIM:]
    return jnp.concatenate([t1 * c - t2 * s, t2 * c + t1 * s, rest], axis=-1)

def rglru_branch(xr, gr, conv_w, conv_b, w_rg, b_rg, w_ig, b_ig, lru_lambda):
    B, S, _ = xr.shape
    xp = jnp.pad(xr, ((0, 0), (CONV_WIDTH - 1, 0), (0, 0)))
    xc = conv_b
    for k in range(CONV_WIDTH):
        xc = xc + xp[:, k:k + S] * conv_w[k]
    xb = xc.reshape(B, S, RNN_BLOCKS, RNN_BLOCK)
    r = jax.nn.sigmoid(jnp.einsum('bsnc,ncd->bsnd', xb, w_rg).reshape(B, S, RNN_WIDTH) + b_rg)
    i = jax.nn.sigmoid(jnp.einsum('bsnc,ncd->bsnd', xb, w_ig).reshape(B, S, RNN_WIDTH) + b_ig)
    log_a = -LRU_C * r.astype(jnp.float32) * jax.nn.softplus(-lru_lambda.astype(jnp.float32))
    a = jnp.exp(log_a)
    mult = jnp.sqrt(-jnp.expm1(2.0 * log_a))
    b_in = mult * (i * xc).astype(jnp.float32)

    def combine(lhs, rhs):
        a1, b1 = lhs
        a2, b2 = rhs
        return a1 * a2, a2 * b1 + b2

    _, h = lax.associative_scan(combine, (a, b_in), axis=1)
    return h.astype(xr.dtype) * jax.nn.gelu(gr)

def swa_sink_branch(q, k, v, sinks, cos, sin):
    B, S, _ = q.shape
    NB = S // BLOCK
    q = apply_partial_rope(q.reshape(B, S, N_Q_HEADS, HEAD_DIM), cos, sin)
    k = apply_partial_rope(k.reshape(B, S, N_KV_HEADS, HEAD_DIM), cos, sin)
    v = v.reshape(B, S, N_KV_HEADS, HEAD_DIM)
    qb = q.reshape(B, NB, BLOCK, N_KV_HEADS, GROUP, HEAD_DIM)

    def band(t):
        tp = jnp.pad(t, ((0, 0), (BLOCK, 0), (0, 0), (0, 0))).reshape(B, NB + 1, BLOCK, N_KV_HEADS, HEAD_DIM)
        return jnp.concatenate([tp[:, :-1], tp[:, 1:]], axis=2)

    kb, vb = band(k), band(v)
    scores = jnp.einsum('bnqhgd,bnjhd->bnhgqj', qb, kb).astype(jnp.float32) * (HEAD_DIM ** -0.5)
    blk = jnp.arange(NB)[:, None, None]
    qpos = blk * BLOCK + jnp.arange(BLOCK)[None, :, None]
    kpos = (blk - 1) * BLOCK + jnp.arange(2 * BLOCK)[None, None, :]
    valid = (kpos <= qpos) & (kpos > qpos - WINDOW) & (kpos >= 0)
    scores = jnp.where(valid[None, :, None, None], scores, NEG_INF)
    sink = sinks.astype(jnp.float32).reshape(N_KV_HEADS, GROUP)[None, None, :, :, None, None]
    sink = jnp.broadcast_to(sink, scores.shape[:-1] + (1,))
    probs = jax.nn.softmax(jnp.concatenate([scores, sink], axis=-1), axis=-1)[..., :-1]
    out = jnp.einsum('bnhgqj,bnjhd->bnqhgd', probs.astype(vb.dtype), vb)
    return out.reshape(B, S, ATTN_WIDTH)

def hybrid_mixer(u, w_in, conv_w, conv_b, w_rg, b_rg, w_ig, b_ig, lru_lambda,
                 w_br_rnn, w_br_attn, sinks, w_out, cos, sin):
    widths = (RNN_WIDTH, RNN_WIDTH, ATTN_WIDTH, KV_WIDTH, KV_WIDTH, D_MODEL, D_MODEL)
    points = np.cumsum(widths)[:-1].tolist()
    proj = u @ w_in
    xr, gr, q, k, v, g_rnn, g_attn = jnp.split(proj, points, axis=-1)
    y_rnn = rglru_branch(xr, gr, conv_w, conv_b, w_rg, b_rg, w_ig, b_ig, lru_lambda)
    y_attn = swa_sink_branch(q, k, v, sinks, cos, sin)
    merged = jax.nn.sigmoid(g_rnn) * (y_rnn @ w_br_rnn) + jax.nn.sigmoid(g_attn) * (y_attn @ w_br_attn)
    return merged @ w_out

def cross_attention(u, mem, cq_w, ckv_w, co_w):
    B, S, _ = u.shape
    M = mem.shape[1]
    q = (u @ cq_w).reshape(B, S, CROSS_HEADS, CROSS_HEAD_DIM)
    k, v = jnp.split(mem @ ckv_w, 2, axis=-1)
    k = k.reshape(B, M, CROSS_HEADS, CROSS_HEAD_DIM)
    v = v.reshape(B, M, CROSS_HEADS, CROSS_HEAD_DIM)
    s = jnp.einsum('bshd,bmhd->bhsm', q, k).astype(jnp.float32) * (CROSS_HEAD_DIM ** -0.5)
    p = jax.nn.softmax(s, axis=-1)
    o = jnp.einsum('bhsm,bmhd->bshd', p.astype(v.dtype), v).reshape(B, S, CROSS_WIDTH)
    return o @ co_w

def swiglu(u, wi, wo):
    gate, up = jnp.split(u @ wi, 2, axis=-1)
    return (jax.nn.silu(gate) * up) @ wo

def second_inputs(seed: int = 0) -> dict:
    key = jax.random.key(seed)
    ks = jax.random.split(key, 26)
    L = DEPTH_2
    f32 = jnp.float32

    def nrm(k, shape, scale):
        return jax.random.normal(k, shape, f32) * scale

    u = jax.random.uniform(ks[9], (L, RNN_WIDTH), f32, 0.9, 0.999)
    p = u ** (1.0 / LRU_C)
    lru_lambda = jnp.log(p) - jnp.log1p(-p)
    return {
        "x": nrm(ks[0], (BATCH, SEQ, D_MODEL), 1.0),
        "mem": nrm(ks[1], (BATCH, MEM_LEN, D_MODEL), 1.0),
        "w_in": nrm(ks[2], (L, D_MODEL, IN_COLS), D_MODEL ** -0.5),
        "conv_w": nrm(ks[3], (L, CONV_WIDTH, RNN_WIDTH), CONV_WIDTH ** -0.5),
        "conv_b": nrm(ks[4], (L, RNN_WIDTH), 0.01),
        "w_rg": nrm(ks[5], (L, RNN_BLOCKS, RNN_BLOCK, RNN_BLOCK), RNN_BLOCK ** -0.5),
        "b_rg": nrm(ks[6], (L, RNN_WIDTH), 0.01),
        "w_ig": nrm(ks[7], (L, RNN_BLOCKS, RNN_BLOCK, RNN_BLOCK), RNN_BLOCK ** -0.5),
        "b_ig": nrm(ks[8], (L, RNN_WIDTH), 0.01),
        "lru_lambda": lru_lambda,
        "w_br_rnn": nrm(ks[10], (L, RNN_WIDTH, D_MODEL), RNN_WIDTH ** -0.5),
        "w_br_attn": nrm(ks[11], (L, ATTN_WIDTH, D_MODEL), ATTN_WIDTH ** -0.5),
        "sinks": nrm(ks[12], (L, N_Q_HEADS), 0.5),
        "w_out": nrm(ks[13], (L, D_MODEL, D_MODEL), DEEPNORM_BETA * D_MODEL ** -0.5),
        "ln1_g": 1.0 + nrm(ks[14], (L, D_MODEL), 0.02),
        "ln1_b": nrm(ks[15], (L, D_MODEL), 0.02),
        "cq_w": nrm(ks[16], (L, D_MODEL, CROSS_WIDTH), D_MODEL ** -0.5),
        "ckv_w": nrm(ks[17], (L, D_MODEL, 2 * CROSS_WIDTH), D_MODEL ** -0.5),
        "co_w": nrm(ks[18], (L, CROSS_WIDTH, D_MODEL), DEEPNORM_BETA * CROSS_WIDTH ** -0.5),
        "ln2_g": 1.0 + nrm(ks[19], (L, D_MODEL), 0.02),
        "ln2_b": nrm(ks[20], (L, D_MODEL), 0.02),
        "ffn_wi": nrm(ks[21], (L, D_MODEL, 2 * D_FF), D_MODEL ** -0.5),
        "ffn_wo": nrm(ks[22], (L, D_FF, D_MODEL), DEEPNORM_BETA * D_FF ** -0.5),
        "ln3_g": 1.0 + nrm(ks[23], (L, D_MODEL), 0.02),
        "ln3_b": nrm(ks[24], (L, D_MODEL), 0.02),
    }

def second_block(x, mem, w_in, conv_w, conv_b, w_rg, b_rg, w_ig, b_ig, lru_lambda,
              w_br_rnn, w_br_attn, sinks, w_out, ln1_g, ln1_b,
              cq_w, ckv_w, co_w, ln2_g, ln2_b,
              ffn_wi, ffn_wo, ln3_g, ln3_b):
    cos, sin = rope_tables_2(x.shape[1])
    h = x
    for l in range(DEPTH_2):
        mix = hybrid_mixer(h, w_in[l], conv_w[l], conv_b[l], w_rg[l], b_rg[l], w_ig[l], b_ig[l],
                           lru_lambda[l], w_br_rnn[l], w_br_attn[l], sinks[l], w_out[l], cos, sin)
        h = layer_norm_2(DEEPNORM_ALPHA * h + mix, ln1_g[l], ln1_b[l])
        h = layer_norm_2(DEEPNORM_ALPHA * h + cross_attention(h, mem, cq_w[l], ckv_w[l], co_w[l]),
                       ln2_g[l], ln2_b[l])
        h = layer_norm_2(DEEPNORM_ALPHA * h + swiglu(h, ffn_wi[l], ffn_wo[l]), ln3_g[l], ln3_b[l])
    return h


def setup_inputs(seed=0):
    out = dict(first_inputs(seed))
    for name, value in second_inputs(seed + 1).items():
        if name != "x":
            out[name + "_2"] = value
    return out


def reference(
    x, w_in, conv_w, conv_b, dt_bias, a_log, d_skip, ssd_norm_w, w_out, ln1_g, ln1_b,
    w_route_group, b_route_group, w_route_expert, b_route_expert, w_gate, w_up, w_down, ln2_g,
    ln2_b, mem_2, w_in_2, conv_w_2, conv_b_2, w_rg_2, b_rg_2, w_ig_2, b_ig_2, lru_lambda_2,
    w_br_rnn_2, w_br_attn_2, sinks_2, w_out_2, ln1_g_2, ln1_b_2, cq_w_2, ckv_w_2, co_w_2,
    ln2_g_2, ln2_b_2, ffn_wi_2, ffn_wo_2, ln3_g_2, ln3_b_2,
):
    x = first_block(
        x, w_in, conv_w, conv_b, dt_bias, a_log, d_skip, ssd_norm_w, w_out, ln1_g, ln1_b,
        w_route_group, b_route_group, w_route_expert, b_route_expert, w_gate, w_up, w_down,
        ln2_g, ln2_b,
    )
    return second_block(
        x, mem_2, w_in_2, conv_w_2, conv_b_2, w_rg_2, b_rg_2, w_ig_2, b_ig_2, lru_lambda_2,
        w_br_rnn_2, w_br_attn_2, sinks_2, w_out_2, ln1_g_2, ln1_b_2, cq_w_2, ckv_w_2, co_w_2,
        ln2_g_2, ln2_b_2, ffn_wi_2, ffn_wo_2, ln3_g_2, ln3_b_2,
    )


_drawn_inputs = setup_inputs


def setup_inputs(seed=0):
    import zlib

    import numpy as np

    out = dict(_drawn_inputs(seed))
    spreads = {}
    factors = {'conv_b': 5.777,
     'b_route_group': 18.599,
     'b_route_expert': 8.0,
     'conv_b_2': 6.6,
     'b_rg_2': 200.0,
     'b_ig_2': 64.0,
     'sinks_2': 24.508}
    for name, (base, spread) in spreads.items():
        noise = np.random.default_rng([zlib.crc32(name.encode()), seed]).standard_normal(out[name].shape)
        drawn = base * np.exp(spread * noise) if base else spread * noise
        out[name] = jnp.asarray(drawn.astype(out[name].dtype))
    for name, factor in factors.items():
        out[name] = (out[name] * factor).astype(out[name].dtype)
    return out
```

```python
from contextlib import ExitStack

import numpy as np
import concourse.bass as bass
from concourse import mybir

ALU = mybir.AluOpType
ACT = mybir.ActivationFunctionType
F32 = mybir.dt.float32
F32R = mybir.dt.float32r
AX = mybir.AxisListType

P = 128
T = 512
NT = T // P
D = 1024
KD = D // P
HD = 64
NEG = -1.0e30
GONE = -3.0e38
EPS = 1e-5

A_HEADS, I_HEADS, TOPK = 8, 4, 128
S_HEADS, S_GROUPS = 8, 2
EXPERTS, GROUPS, FF1 = 16, 4, 256
ALPHA1 = 2 ** 0.25
IDX_SCALE = (I_HEADS ** -0.5) * (HD ** -0.5)
Q0, KV0, IQ0, IK0, Z0, XBC0, DT0 = 0, 512, 640, 896, 964, 1476, 2244
LAYERS, MEM = 2, 256
ALPHA2 = 4 ** 0.25
Q_HEADS2, KV_HEADS2, X_HEADS = 16, 2, 4
FF2 = 2816
XR0, GR0, QQ0, KK0, VV0, GRNN0, GATT0 = 0, 1024, 2048, 3072, 3200, 3328, 4352

SLAB, RING = 1024, 3
N_FIRST = 28
N_EXPERT = 6
N_LAYER = 168
FF_HALVES = ((0, 12), (12, 10))
L_BASE = N_FIRST + N_EXPERT * EXPERTS
SLABS = L_BASE + LAYERS * N_LAYER

CONSTS = [("ident", 128), ("rot1", 128), ("dup", 128), ("duprot", 128), ("rot2", 128), ("swap", 128),
          ("tri", 128), ("cmask", 128), ("cmask_t", 128), ("swamask", 256), ("one", 128),
          ("cos1", T), ("sin1", T), ("cos2", T), ("sin2", T)]
NCONST = sum(n for _, n in CONSTS)

LAYER_BARRIERS = 20

PHASE_SEMS = ("params_landed", "act_link", "dve_link",
              "products",
              "evacuated",
              "banks_read",
              "transposed", "hi_ready", "lo_ready", "chunk_ready",
              "turned",
              "scores", "scores_read", "maxima", "probs", "sink_exp", "probs_t", "probs_t_copied", "values", "values_read",
              "summed", "variance", "deviation", "normalised",
              "relu", "relu_used", "dt_products",
              "taps0", "convolved", "activated", "sp_in", "sp_exp", "sp_sum", "sp_log", "sp_done",
              "cumulated", "decay_in", "decays", "tokens_x",
              "cb_products", "decay_masked", "decay_exp", "decayed", "chunk_products", "state_ready",
              "square_sum", "gate_in", "gate_exp",
              "gates_full", "ups_full", "silu_done", "hidden", "hidden_hi", "hidden_lo", "downs_full", "downs_free",
              "r_done", "i_done", "i_used", "tanh_done", "decay_done", "mult2", "mult", "gelu_done")


def tables():
    c = {}
    eye = np.eye(P, dtype=np.float32)
    c["ident"] = eye
    rot1, rot2, dup, swap = (np.zeros((P, P), np.float32) for _ in range(4))
    for m in range(P):
        d = m % HD
        if d < 32:
            rot1[m + 32, m] = -1.0
        else:
            rot1[m - 32, m] = 1.0
        if d < 8:
            rot2[m + 8, m] = -1.0
        elif d < 16:
            rot2[m - 8, m] = 1.0
        dup[d, m] = 1.0
        swap[(m + HD) % P, m] = 1.0
    c["rot1"], c["rot2"], c["dup"], c["swap"], c["duprot"] = rot1, rot2, dup, swap, dup @ rot1
    i, j = np.arange(P)[:, None], np.arange(P)[None, :]
    c["tri"] = (i <= j).astype(np.float32)
    c["cmask"] = np.where(j <= i, 0.0, NEG).astype(np.float32)
    c["cmask_t"] = np.where(j >= i, 0.0, NEG).astype(np.float32)
    w = np.arange(2 * P)[None, :]
    c["swamask"] = np.where((w > i) & (w <= i + P), 0.0, NEG).astype(np.float32)
    c["one"] = np.ones((P, P), np.float32)
    pos = np.arange(T, dtype=np.float32)
    inv1 = np.float32(10000.0) ** (-np.arange(0, HD, 2, dtype=np.float32) / np.float32(HD))
    ang1 = (pos[:, None] * inv1[None, :]).astype(np.float32)
    c["cos1"] = np.cos(ang1).T[np.arange(P) % 32].astype(np.float32)
    c["sin1"] = np.sin(ang1).T[np.arange(P) % 32].astype(np.float32)
    inv2 = np.float32(500000.0) ** (-np.arange(0, 16, 2, dtype=np.float32) / np.float32(16))
    ang2 = (pos[:, None] * inv2[None, :]).astype(np.float32)
    turned = (np.arange(P) % HD < 16)[:, None]
    c["cos2"] = np.where(turned, np.cos(ang2).T[np.arange(P) % 8], 1.0).astype(np.float32)
    c["sin2"] = np.where(turned, np.sin(ang2).T[np.arange(P) % 8], 0.0).astype(np.float32)
    return np.ascontiguousarray(np.concatenate([c[n] for n, _ in CONSTS], axis=1))


def build(nc, A, out):
    KB = 1024
    top = [(nc.sbuf_base + 63) // 64 * 64]

    def place(name, shape, dtype=F32, offset=None):
        size = 4 * int(np.prod(shape[1:]))
        if offset is None:
            offset, top[0] = top[0], (top[0] + size + 63) // 64 * 64
        else:
            offset = arena + offset * KB
        return nc.alloc_sbuf_tensor_at(name, shape, dtype, offset=offset)

    w_raw = place("w_raw", [P, RING, SLAB])
    w_hi = place("w_hi", [P, RING, SLAB], F32R)
    w_lo = place("w_lo", [P, RING, SLAB], F32R)
    res = place("res", [P, NT, D])
    x_hi = place("x_hi", [P, KD, T], F32R)
    x_lo = place("x_lo", [P, KD, T], F32R)
    const = place("const", [P, NCONST])
    gain = place("gain", [P, 2, D])
    gain_f = place("gain_f", [P, 2, KD])
    taps = place("taps", [P, 4, KD])
    tap_bias = place("tap_bias", [P, KD])
    gate_bias = place("gate_bias", [P, 2, KD])
    lam = place("lam", [P, 8, KD])
    sink = place("sink", [P, Q_HEADS2])
    stats = place("stats", [P, NT, 2, 6])
    mv = place("mv", [P, NT, 2])
    dev = place("dev", [P, NT])
    rdev = place("rdev", [P, NT])
    nmax = place("nmax", [P, 2, 2])
    den = place("den", [P, 2, 2])
    esink = place("esink", [P, 2, 2])
    rden = place("rden", [P, 2, 2])
    vbuf = place("vbuf", [P, 2, T])
    iw = place("iw", [P, NT, I_HEADS])
    top8 = place("top8", [P, 8])
    short = place("short", [P, 1])
    sp = place("sp", [P, 8, 32])
    dt_raw = place("dt_raw", [P, 32])
    dt_a = place("dt_a", [P, 32])
    head_in = place("head_in", [P, 4, 8])
    norm_w = place("norm_w", [P, 4])
    dec = place("dec", [P, 6, 32])
    dec_t = place("dec_t", [P, 32])
    dec4 = place("dec4", [P, NT, 4])
    route_b = place("route_b", [P, 20])
    rt = place("rt", [P, NT, 64])
    gates = place("gates", [P, NT, EXPERTS])
    arena = top[0]
    consts = {}
    at = 0
    for name, width in CONSTS:
        consts[name] = const[:, at:at + width]
        at += width
    ident = consts["ident"]
    ps = nc.alloc_psum_tensor("ps", [P, 8, 512], F32)

    pf = place("pf", [P, 14, T], F32, 0)
    zt = place("zt", [P, NT, 512], F32, 30)
    mb = place("mb", [P, NT, T], F32, 38)
    sc1 = place("sc1", [P, 2, 2, T], F32, 46)
    pt1 = place("pt1", [P, 2, 2, T], F32, 54)
    ot1 = place("ot1", [P, NT, D], F32, 62)
    vt1 = place("vt1", [P, NT, HD], F32, 78)
    ix = place("ix", [P, 4, T], F32, 46)
    rl = place("rl", [P, 4, T], F32, 54)
    ones = place("ones", [P, T], F32, 62)
    xc1 = place("xc1", [P, 6, T], F32, 79)
    xt1 = place("xt1", [P, NT, 512], F32, 46)
    bt1 = place("bt1", [P, NT, P], F32, 54)
    xdt = place("xdt", [P, NT, 512], F32, 0)
    lm = place("lm", [P, 2, 4, P], F32, 8)
    prev = place("prev", [P, 256], F32, 12)
    yt = place("yt", [P, 512], F32, 13)
    xsk = place("xsk", [P, NT, 512], F32, 16)
    sq = place("sq", [P, 512], F32, 24)
    xdec = place("xdec", [P, NT, 512], F32, 38)
    oh1 = place("oh1", [P, KD, T], F32R, 0)
    ol1 = place("ol1", [P, KD, T], F32R, 16)
    eh = place("eh", [P, 2, T], F32R, 0)
    el = place("el", [P, 2, T], F32R, 4)
    esg = place("esg", [P, 2, T], F32, 8)
    ehd = place("ehd", [P, 2, T], F32, 12)
    qf = place("qf", [P, 8, T], F32, 0)
    kr = place("kr", [P, T], F32, 16)
    ks = place("ks", [P, 2, T], F32, 18)
    vr = place("vr", [P, T], F32, 22)
    vt2 = place("vt2", [P, NT, P], F32, 24)
    sc2 = place("sc2", [P, 2, 2, 256], F32, 26)
    pt2 = place("pt2", [P, 2, 2, 256], F32, 30)
    ot2 = place("ot2", [P, NT, D], F32, 34)
    oh2 = place("oh2", [P, KD, T], F32R, 50)
    ol2 = place("ol2", [P, KD, T], F32R, 66)
    sgm = place("sgm", [P, 2, T], F32, 82)
    mg = place("mg", [P, KD, T], F32, 0)
    xc2 = place("xc2", [P, KD, T], F32, 16)
    yh = place("yh", [P, KD, T], F32R, 34)
    yl = place("yl", [P, KD, T], F32R, 50)
    ga = place("ga", [P, KD, T], F32, 66)
    t8 = place("t8", [P, KD, T], F32, 34)
    t4 = place("t4", [P, 4, T], F32, 82)
    mh = place("mh", [P, KD, T], F32R, 66)
    ml = place("ml", [P, KD, T], F32R, 16)
    mt = place("mt", [P, 2, D], F32, 0)
    mem_h = place("mem_h", [P, KD, MEM], F32R, 8)
    mem_l = place("mem_l", [P, KD, MEM], F32R, 16)
    kc = place("kc", [P, KD, MEM], F32, 24)
    vc = place("vc", [P, 2, D], F32, 32)
    qc = place("qc", [P, KD, T], F32, 40)
    sc3 = place("sc3", [P, 2, 2, 256], F32, 56)
    pt3 = place("pt3", [P, 2, 2, 256], F32, 60)
    ot3 = place("ot3", [P, NT, D], F32, 64)
    oh3 = place("oh3", [P, KD, T], F32R, 0)
    ol3 = place("ol3", [P, KD, T], F32R, 16)
    fh = place("fh", [P, 12, T], F32R, 0)
    fl = place("fl", [P, 12, T], F32R, 24)
    fsg = place("fsg", [P, 2, 2, T], F32, 48)
    fhd = place("fhd", [P, 2, T], F32, 56)

    UNITS1 = [(i, p) for i in range(NT) for p in range(A_HEADS // 2)]
    UNITS2 = [(i, p) for i in range(NT) for p in range(Q_HEADS2 // 2)]
    UNITS3 = [(i, p) for i in range(NT) for p in range(X_HEADS // 2)]

    def width1(unit):
        return (unit[0] + 1) * P

    def width2(unit):
        return 2 * P if unit[0] else P

    def width3(unit):
        return MEM

    with ExitStack() as ctx:
        def sem(name):
            return ctx.enter_context(nc.semaphore(name))

        s = {name: sem(name) for name in PHASE_SEMS}
        nums = sorted(v.num for v in s.values())
        assert nums == list(range(nums[0], nums[0] + len(nums)))
        phase_range = range(nums[0], nums[-1] + 1)
        raw_landed = [sem(f"raw_landed{i}") for i in range(RING)]
        hi_done, lo_done, slab_used = sem("hi_done"), sem("lo_done"), sem("slab_used")
        arrived, stored, start, loads_begun = sem("arrived"), sem("stored"), sem("start"), sem("loads_begun")
        go = [sem("go_even"), sem("go_odd")]
        finished = sem("finished")
        block = ctx.enter_context(nc.Block())

        class Count:
            def __init__(self):
                self.n, self.base, self.turns, self.looped = 0, 0, 0, False

            def at(self, more):
                return self.base + (self.n + more) if self.looped else self.n + more

            def enter(self, base, turns=0):
                self.base, self.turns, self.looped = base, turns, True

            def leave(self):
                self.base, self.turns, self.looped = 0, 0, False

        def view(w):
            return w.rearrange("(k p) n -> p k n", p=P)

        def f_pair(v, c0, width=256):
            for h in range(2):
                yield v[:, 4 * h:4 * h + 4, c0:c0 + width]

        def rows(v, ks_, c0=0):
            for k in ks_:
                yield v[:, k:k + 1, c0:c0 + D]

        def slabs_first():
            w = view(A["w_in"][0])
            for c0, n in ((Q0, 256), (Q0 + 256, 256), (KV0, 256), (IQ0 + 128, 196)):
                yield from f_pair(w, c0, n)
            for c0 in (XBC0, XBC0 + 256, XBC0 + 512):
                yield from f_pair(w, c0)
            yield w[:, :, DT0:DT0 + 8]
            for h in range(4):
                yield w[:, 2 * h:2 * h + 2, Z0:Z0 + 512]
            yield from rows(view(A["w_out"][0]), range(KD))
            yield view(A["w_route"][0])

        def expert_up(e):
            for w in (A["w_gate"], A["w_up"]):
                yield from f_pair(view(w[0][e]), 0)

        def expert_down(e):
            v = view(A["w_down"][0][e])
            for h in range(2):
                yield v[:, :, 512 * h:512 * h + 512]

        def layer_slabs(l):
            w = view(A["w_in_2"][l])
            for c0 in [*range(QQ0, KK0, 256), KK0]:
                yield from f_pair(w, c0)
            for p in range(4):
                yield from f_pair(w, GATT0 + 256 * p)
                yield from f_pair(view(A["w_br_attn_2"][l]), 256 * p)
            for p in range(4):
                yield from f_pair(w, XR0 + 256 * p)
            for name in ("w_rg_2", "w_ig_2"):
                v = A[name][l].rearrange("b (k p) n -> p (b k) n", p=P)
                for h in range(2):
                    yield v[:, 4 * h:4 * h + 4, :]
            for p in range(4):
                yield from f_pair(w, GR0 + 256 * p)
            for p in range(4):
                yield from f_pair(w, GRNN0 + 256 * p)
                yield from f_pair(view(A["w_br_rnn_2"][l]), 256 * p)
            yield from rows(view(A["w_out_2"][l]), range(KD))
            for p in range(4):
                yield from f_pair(view(A["ckv_w_2"][l]), 256 * p)
            yield from rows(view(A["ckv_w_2"][l]), range(KD), D)
            for p in range(4):
                yield from f_pair(view(A["cq_w_2"][l]), 256 * p)
            yield from rows(view(A["co_w_2"][l]), range(KD))
            wi, wo = view(A["ffn_wi_2"][l]), view(A["ffn_wo_2"][l])
            for c0, n in FF_HALVES:
                for p in range(n // 2):
                    yield from f_pair(wi, 128 * c0 + 256 * p)
                    yield from f_pair(wi, FF2 + 128 * c0 + 256 * p)
                yield from rows(wo, range(c0, c0 + n))

        @block.sync
        def _(sync):
            slab = Count()

            def load(src):
                slot = slab.n % RING
                if slab.looped or slab.n >= RING:
                    sync.wait_ge(lo_done, slab.at(1 - RING))
                    if slab.looped:
                        sync.sem_inc(loads_begun, 1)
                k, n = src.shape[1], src.shape[2]
                sync.dma_start(w_raw[:, slot, :k * n].rearrange("p (k n) -> p k n", k=k), src)\
                    .then_inc(raw_landed[slot], 16)
                slab.n += 1

            for src in [*slabs_first(), *expert_up(0)]:
                load(src)
            assert slab.n == N_FIRST + 4
            with sync.Fori(0, EXPERTS - 1) as e:
                slab.enter(e * N_EXPERT)
                for src in [*expert_up(e + 1), *expert_down(e)]:
                    load(src)
            slab.leave()
            slab.n += (EXPERTS - 2) * N_EXPERT
            for src in expert_down(EXPERTS - 1):
                load(src)
            assert slab.n == L_BASE
            with sync.Fori(0, LAYERS) as l:
                slab.enter(l * N_LAYER)
                for src in layer_slabs(l):
                    load(src)
            assert slab.n == L_BASE + N_LAYER, slab.n
            sync.wait_ge(finished, 1)
            sync.dma_start(out[0].rearrange("(t p) d -> p t d", p=P), res[:, :, :]).then_inc(stored, 16)
            sync.wait_ge(stored, 16)

        @block.gpsimd
        def _(pool):
            def low(slot, value):
                pool.wait_ge(hi_done, value)
                pool.tensor_tensor(w_lo[:, slot, :], w_raw[:, slot, :], w_hi[:, slot, :].bitcast(F32),
                                   ALU.subtract).then_inc(lo_done, 1)

            with pool.Fori(0, SLABS // RING) as g:
                for i in range(RING):
                    low(i, g * RING + (i + 1))
            for n in range(SLABS // RING * RING, SLABS):
                low(n % RING, n + 1)

        @block.tensor
        def _(pe):
            slab, phase = Count(), Count()
            used_later = [False]

            def mm(o, a, b, first=True, last=True, inc=None):
                ins = pe.matmul(o, a, b, start=first, stop=last)
                if inc is not None:
                    assert not used_later[0]
                    ins.then_inc(s[inc], 1)
                elif used_later[0]:
                    ins.then_inc(slab_used, 1)
                    used_later[0] = False
                return ins

            def flip(o, a, inc=None):
                n = a.shape[0]
                ins = pe.transpose(o, a, ident[:n, :n])
                if inc is not None:
                    assert not used_later[0]
                    ins.then_inc(s[inc], 1)
                elif used_later[0]:
                    ins.then_inc(slab_used, 1)
                    used_later[0] = False

            def flush():
                if used_later[0]:
                    pe.drain().then_inc(slab_used, 1)
                    used_later[0] = False

            def barrier():
                flush()
                pe.drain().then_inc(arrived, 1)
                pe.wait_ge(go[phase.n % 2], 1)
                pe.drain()
                phase.n += 1

            def take():
                pe.wait_ge(lo_done, slab.at(1))
                slab.n += 1
                return (slab.n - 1) % RING

            def three(o, ah, al, bh, bl, first, last, inc=None):
                mm(o, ah, bh, first, False)
                mm(o, al, bh, False, False)
                return mm(o, ah, bl, False, last, inc)

            def three_t(o, xh, xl, wh, wl, first, last, inc=None):
                mm(o, xh, wh, first, False)
                mm(o, xh, wl, False, False)
                return mm(o, xl, wh, False, last, inc)

            def pair_f(banks, xh, xl, width=256, nt=T, inc="products"):
                for h in range(2):
                    slot = take()
                    for c, m in enumerate((P, width - P)):
                        for kk in range(4):
                            k, col, end = 4 * h + kk, kk * width + c * P, kk == 3
                            ins = three(ps[:m, banks[c], 0:nt], w_hi[:, slot, col:col + m], w_lo[:, slot, col:col + m],
                                        xh[:, k, 0:nt], xl[:, k, 0:nt], k == 0, k == 7,
                                        inc if (h == 1 and end) else None)
                            if h == 0 and end and c == 1:
                                ins.then_inc(slab_used, 1)
                used_later[0] = True

            def rows_t(xh, xl, n, tiles=NT):
                for k in range(n):
                    slot = take()
                    for t in range(tiles):
                        for half in range(2):
                            tk, wk = slice(t * P, t * P + P), slice(512 * half, 512 * half + 512)
                            ins = three_t(ps[:, 2 * t + half, :], xh[:, k, tk], xl[:, k, tk],
                                          w_hi[:, slot, wk], w_lo[:, slot, wk], k == 0, k == n - 1,
                                          "products" if (k == n - 1 and half == 1) else None)
                    if k < n - 1:
                        ins.then_inc(slab_used, 1)
                used_later[0] = True

            def narrow_t(bank, width, step, inc):
                slot = take()
                for t in range(NT):
                    for k in range(KD):
                        tk, wk = slice(t * P, t * P + P), slice(k * width, k * width + width)
                        three_t(ps[:, bank, t * step:t * step + width], x_hi[:, k, tk], x_lo[:, k, tk],
                                w_hi[:, slot, wk], w_lo[:, slot, wk], k == 0, k == KD - 1,
                                inc if (t == NT - 1 and k == KD - 1) else None)
                used_later[0] = True

            def to_features(src, tiles=NT):
                for k in range(KD):
                    for t in range(tiles):
                        flip(ps[:, k, t * P:t * P + P], src[:, t, k * P:k * P + P],
                             "transposed" if t == tiles - 1 else None)

            def normed_to_features():
                flush()
                pe.wait_ge(s["summed"], NT)
                for t in range(NT):
                    pe.wait_ge(s["normalised"], t + 1)
                    for k in range(KD):
                        flip(ps[:, k, t * P:t * P + P], res[:, t, k * P:k * P + P],
                             "transposed" if t == NT - 1 else None)

            def attention(units, width, sc, pt, scores_of, values_of):
                def scores(u):
                    if u >= 2:
                        pe.wait_ge(s["scores_read"], u - 1)
                    scores_of(u, units[u])

                scores(0)
                for u, unit in enumerate(units):
                    n = width(unit) // P
                    if u + 1 < len(units):
                        scores(u + 1)
                    pe.wait_ge(s["probs"], 2 * u + 2)
                    if u >= 1:
                        pe.wait_ge(s["probs_t_copied"], u)
                    for h in range(2):
                        for j in range(n):
                            flip(ps[:, 4 + h, j * P:j * P + P], sc[:, u % 2, h, j * P:j * P + P],
                                 "probs_t" if (h == 1 and j == n - 1) else None)
                    pe.wait_ge(s["probs_t_copied"], u + 1)
                    if u >= 2:
                        pe.wait_ge(s["values_read"], u - 1)
                    for h in range(2):
                        for j in range(n):
                            v = values_of(unit, h, j)
                            dv = v.shape[-1]
                            mm(ps[:, 6 + u % 2, h * dv:h * dv + dv], pt[:, u % 2, h, j * P:j * P + P], v,
                               j == 0, j == n - 1, "values" if (h == 1 and j == n - 1) else None)

            pe.wait_ge(start, 16 * 2)
            to_features(res)
            barrier()
            for p in range(4):
                pair_f((2 * p, 2 * p + 1), x_hi, x_lo, 196 if p == 3 else 256)
            barrier()
            for j, c in enumerate((0, 1, 2, 3, 5, 6)):
                mm(ps[:, j, :], consts["rot1"], pf[:, c, :], inc="products")
            mm(ps[:, 6, :], consts["dup"], pf[:, 4, :], inc="products")
            mm(ps[:, 7, :], consts["duprot"], pf[:, 4, :], inc="products")
            pe.wait_ge(s["banks_read"], 1)
            mm(ps[:, 0, :], consts["dup"][:68, :], pf[:68, 7, :], inc="products")
            pe.wait_ge(s["banks_read"], 2)
            mm(ps[:, 1, :], consts["duprot"][:68, :], pf[:68, 7, :], inc="products")
            pe.wait_ge(s["banks_read"], 3)
            for t in range(NT):
                flip(ps[:, 2, t * P:t * P + P], pf[:, 4, t * P:t * P + P], "products" if t == NT - 1 else None)
            pe.wait_ge(s["banks_read"], 4)
            for t in range(NT):
                flip(ps[:, 3, t * P:t * P + 68], pf[:68, 7, t * P:t * P + P], "products" if t == NT - 1 else None)
            barrier()
            for i in range(1, NT):
                for h in range(I_HEADS):
                    b = HD * (h % 2)
                    if i >= 2:
                        pe.wait_ge(s["relu"], 4 * (i - 2) + h + 1)
                    mm(ps[:, h, 0:(i + 1) * P], pf[b:b + HD, 5 + h // 2, i * P:i * P + P],
                       pf[b:b + HD, 7, 0:(i + 1) * P], inc="scores")
            pe.wait_ge(s["relu"], 4 * (NT - 1))
            for p in range(3):
                pair_f((2 * p, 2 * p + 1), x_hi, x_lo)
            narrow_t(6, 8, 8, "dt_products")
            pe.wait_ge(s["evacuated"], 4)
            for j in range(4):
                slot = take()
                for t in range(NT):
                    for kk in range(2):
                        k, tk, wk = 2 * j + kk, slice(t * P, t * P + P), slice(kk * 512, kk * 512 + 512)
                        ins = three_t(ps[:, t, :], x_hi[:, k, tk], x_lo[:, k, tk], w_hi[:, slot, wk],
                                      w_lo[:, slot, wk], k == 0, k == 7, "products" if k == 7 else None)
                if j < 3:
                    ins.then_inc(slab_used, 1)
            used_later[0] = True
            barrier()

            def scores1(u, unit):
                i, p = unit
                for h in range(2):
                    b = HD * h
                    mm(ps[:, 2 * (u % 2) + h, 0:width1(unit)], pf[b:b + HD, p, i * P:i * P + P],
                       pf[b:b + HD, 4, 0:width1(unit)], inc="scores" if h == 1 else None)

            attention(UNITS1, width1, sc1, pt1, scores1, lambda unit, h, j: vt1[:, j, :])
            barrier()
            for c in range(5):
                pe.wait_ge(s["activated"], c + 1)
                for t in range(NT):
                    flip(ps[:, c, t * P:t * P + P], xc1[:, c, t * P:t * P + P], "transposed" if t == NT - 1 else None)
            pe.wait_ge(s["sp_done"], 1)
            mm(ps[:, 5, 0:32], consts["tri"], dt_a[:, :])
            mm(ps[:, 6, 0:32], consts["one"], dt_a[:, :], inc="cumulated")
            barrier()
            for c in range(NT):
                tk = slice(c * P, c * P + P)
                for g in range(S_GROUPS):
                    j = 2 * c + g
                    r = slice(HD * g, HD * g + HD)
                    if c >= 1:
                        pe.wait_ge(s["decayed"], j - 1)
                    mm(ps[:, g, 0:P], xc1[r, 4, tk], xc1[r, 5, tk])
                    for h in range(4):
                        col = c * 8 + g * 4 + h
                        mm(ps[:, 2 + g, h * P:h * P + P], dt_a[:, col:col + 1].broadcast_to([P, P]), consts["tri"],
                           inc="cb_products" if h == 3 else None)
                if c >= 1:
                    pe.wait_ge(s["state_ready"], c)
                for g in range(S_GROUPS):
                    r = slice(HD * g, HD * g + HD)
                    mm(ps[:, 5 + 2 * g, 0:256], xc1[r, 5, tk], prev[r, :])
                    mm(ps[r, 6, 0:256], bt1[:, c, g * HD:g * HD + HD], xdec[:, c, g * 256:g * 256 + 256])
                for g in range(S_GROUPS):
                    pe.wait_ge(s["decayed"], 2 * c + g + 1)
                    for h in range(4):
                        q = (g * 4 + h) * HD
                        mm(ps[:, 4, q:q + HD], lm[:, g, h, :], xdt[:, c, q:q + HD],
                           inc="chunk_products" if (h == 3 and g == 1) else None)
            barrier()
            to_features(ot1)
            barrier()
            rows_t(oh1, ol1, KD)
            normed_to_features()
            barrier()
            narrow_t(7, 20, 32, "products")

            def up(e):
                if e is not None:
                    pe.wait_ge(s["silu_done"], 2 * e + 2)
                pair_f((0, 1), x_hi, x_lo, inc="gates_full")
                if e is not None:
                    pe.wait_ge(s["hidden"], 2 * e + 2)
                pair_f((2, 3), x_hi, x_lo, inc="ups_full")

            def down(e):
                flush()
                pe.wait_ge(s["hidden_lo"], 2 * e + 2)
                for half in range(2):
                    slot = take()
                    for t in range(NT):
                        pe.wait_ge(s["downs_free"], 8 * e + (4 * half + t + 1))
                        tk = slice(t * P, t * P + P)
                        for k in range(2):
                            wk = slice(k * 512, k * 512 + 512)
                            three_t(ps[:, 4 + t, :], eh[:, k, tk], el[:, k, tk], w_hi[:, slot, wk], w_lo[:, slot, wk],
                                    k == 0, k == 1, "downs_full" if k == 1 else None)
                    used_later[0] = True

            up(None)
            pe.wait_ge(s["evacuated"], 1)
            pe.sem_inc(s["downs_free"], 4)
            with pe.Fori(0, EXPERTS - 1) as e:
                slab.enter(e * N_EXPERT)
                up(e)
                down(e)
            slab.leave()
            slab.n += (EXPERTS - 2) * N_EXPERT
            down(EXPERTS - 1)
            barrier()
            barrier()

            with pe.Fori(0, LAYERS) as l:
                slab.enter(l * N_LAYER)
                n0, b0 = slab.n, phase.n
                to_features(res)
                barrier()
                for p in range(4):
                    pair_f((2 * p, 2 * p + 1), x_hi, x_lo)
                pe.wait_ge(s["evacuated"], 2)
                pair_f((0, 1), x_hi, x_lo)
                barrier()
                for c in range(8):
                    mm(ps[:, c, :], consts["rot2"], qf[:, c, :], inc="products")
                pe.wait_ge(s["banks_read"], 1)
                mm(ps[:, 0, :], consts["rot2"], kr[:, :], inc="products")
                pe.wait_ge(s["banks_read"], 2)
                for t in range(NT):
                    flip(ps[:, 1, t * P:t * P + P], vr[:, t * P:t * P + P], "products" if t == NT - 1 else None)
                pe.wait_ge(s["turned"], 9)
                mm(ps[:, 2, :], consts["swap"], ks[:, 0, :], inc="products")
                barrier()

                def scores2(u, unit):
                    i, p = unit
                    lo, w = max(i - 1, 0) * P, width2(unit)
                    for h in range(2):
                        b = HD * h
                        mm(ps[:, 2 * (u % 2) + h, 0:w], qf[b:b + HD, p, i * P:i * P + P],
                           ks[b:b + HD, 0 if p // 4 == h else 1, lo:lo + w], inc="scores" if h == 1 else None)

                def values2(unit, h, j):
                    kv = HD * (unit[1] // 4)
                    return vt2[:, max(unit[0] - 1, 0) + j, kv:kv + HD]

                attention(UNITS2, width2, sc2, pt2, scores2, values2)
                barrier()
                to_features(ot2)
                barrier()

                def gated(xh, xl):
                    for p in range(4):
                        b = 4 * (p % 2)
                        if p >= 2:
                            pe.wait_ge(s["evacuated"], 2 * (p - 1))
                        pair_f((b, b + 1), x_hi, x_lo)
                        if p >= 2:
                            pe.wait_ge(s["banks_read"], 2 * (p - 1))
                        pair_f((b + 2, b + 3), xh, xl)

                gated(oh2, ol2)
                barrier()
                for p in range(4):
                    pair_f((2 * p, 2 * p + 1), x_hi, x_lo)
                barrier()
                for g in range(2):
                    for h in range(2):
                        slot = take()
                        for q in range(4):
                            blk, c = q // 2, q % 2
                            j = 4 * h + q
                            if g == 1:
                                pe.wait_ge(s["r_done"], j + 1)
                            for kk in range(2):
                                k, col = 4 * h + 2 * blk + kk, (2 * blk + kk) * 256 + c * P
                                three(ps[:, j, :], w_hi[:, slot, col:col + P], w_lo[:, slot, col:col + P],
                                      yh[:, k, :], yl[:, k, :], kk == 0, kk == 1, "products" if kk == 1 else None)
                        used_later[0] = True
                barrier()
                for p in range(4):
                    pair_f((2 * p, 2 * p + 1), x_hi, x_lo)
                barrier()
                gated(yh, yl)
                barrier()
                rows_t(mh, ml, KD)
                normed_to_features()
                barrier()
                pe.wait_ge(s["params_landed"], 16)
                to_features(mt, tiles=2)
                barrier()
                for p in range(4):
                    pair_f((2 * p, 2 * p + 1), mem_h, mem_l, nt=MEM)
                pe.wait_ge(s["evacuated"], 4)
                rows_t(mem_h, mem_l, KD, tiles=2)
                barrier()
                for p in range(4):
                    pair_f((2 * p, 2 * p + 1), x_hi, x_lo)
                barrier()

                def scores3(u, unit):
                    i, p = unit
                    for h in range(2):
                        for k in range(2):
                            c = 2 * (2 * p + h) + k
                            mm(ps[:, 2 * (u % 2) + h, 0:MEM], qc[:, c, i * P:i * P + P], kc[:, c, :],
                               k == 0, k == 1, "scores" if (h == 1 and k == 1) else None)

                def values3(unit, h, j):
                    head = 2 * unit[1] + h
                    return vc[:, j, 256 * head:256 * head + 256]

                attention(UNITS3, width3, sc3, pt3, scores3, values3)
                barrier()
                to_features(ot3)
                barrier()
                rows_t(oh3, ol3, KD)
                normed_to_features()
                barrier()
                for c0, n in FF_HALVES:
                    for p in range(n // 2):
                        b = 4 * (p % 2)
                        if p >= 2:
                            pe.wait_ge(s["silu_done"], 2 * (p - 1))
                        pair_f((b, b + 1), x_hi, x_lo, inc="gates_full")
                        if p >= 2:
                            pe.wait_ge(s["hidden"], 2 * (p - 1))
                        pair_f((b + 2, b + 3), x_hi, x_lo, inc="ups_full")
                    flush()
                    pe.wait_ge(s["hidden_lo"], n)
                    rows_t(fh, fl, n)
                    barrier()
                barrier()
                assert (slab.n - n0, phase.n - b0) == (N_LAYER, LAYER_BARRIERS), (slab.n - n0, phase.n - b0)

        @block.scalar
        def _(act):
            slab, phase = Count(), Count()
            links = [0]

            def link(ins):
                links[0] += 1
                ins.then_inc(s["act_link"], 1)
                act.wait_ge(s["act_link"], links[0])

            def barrier():
                act.drain().then_inc(arrived, 1)
                act.wait_ge(go[phase.n % 2], 1)
                act.drain()
                phase.n += 1
                links[0] = 0

            def split(count, end=None):
                for _ in range(count):
                    n = slab.n
                    if end is not None and n >= end:
                        return
                    act.wait_ge(raw_landed[n % RING], slab.turns * 16 + 16 * (n // RING + 1))
                    if slab.looped or n >= RING:
                        act.wait_ge(slab_used, slab.at(1 - RING))
                    act.activation(w_hi[:, n % RING, :], w_raw[:, n % RING, :], ACT.Copy).then_inc(hi_done, 1)
                    slab.n += 1

            def load(*pairs):
                for dst, src in pairs:
                    act.dma_start(dst, src).then_inc(s["params_landed"], 16)

            def high_parts(hi, nt=T, affine=None):
                for k in range(KD):
                    act.wait_ge(s["transposed"], k + 1)
                    if affine is None:
                        act.activation(hi[:, k, 0:nt], ps[:, k, 0:nt], ACT.Copy).then_inc(s["hi_ready"], 1)
                        continue
                    g, b = affine(k)
                    if k >= 2:
                        act.wait_ge(s["lo_ready"], k - 1)
                    link(act.activation(vbuf[:, k % 2, 0:nt], ps[:, k, 0:nt], ACT.Identity, scale=g, bias=b))
                    act.activation(hi[:, k, 0:nt], vbuf[:, k % 2, 0:nt], ACT.Copy).then_inc(s["hi_ready"], 1)

            def attention(units, width, sc, pt, sink_of=None):
                def exps(u):
                    w = width(units[u])
                    act.wait_ge(s["maxima"], u + 1)
                    for h in range(2):
                        act.activation(sc[:, u % 2, h, 0:w], sc[:, u % 2, h, 0:w], ACT.Exp,
                                       bias=nmax[:, u % 2, h:h + 1], accum_out=den[:, u % 2, h:h + 1])\
                           .then_inc(s["probs"], 1)
                    if sink_of:
                        for h in range(2):
                            q = sink_of(units[u], h)
                            act.activation(esink[:, u % 2, h:h + 1], sink[:, q:q + 1], ACT.Exp,
                                           bias=nmax[:, u % 2, h:h + 1]).then_inc(s["sink_exp"], 1)

                exps(0)
                for u, unit in enumerate(units):
                    if u + 1 < len(units):
                        exps(u + 1)
                    w = width(unit)
                    act.wait_ge(s["probs_t"], u + 1)
                    if u >= 2:
                        act.wait_ge(s["values"], u - 1)
                    act.activation(pt[:, u % 2, :, 0:w], ps[:, 4:6, 0:w], ACT.Copy).then_inc(s["probs_t_copied"], 1)

            def softplus(e, x, log, u):
                act.wait_ge(s["sp_in"], 1)
                act.activation(e, x, ACT.Exp, scale=-1.0).then_inc(s["sp_exp"], 1)
                act.wait_ge(s["sp_sum"], 1)
                act.activation(log, u, ACT.Ln).then_inc(s["sp_log"], 1)

            def per_feature(name, l):
                return A[name + "_f"][l]

            def load_norm(g, b, l):
                load((gain[:, 0, :], A[g][l].partition_broadcast(P)), (gain[:, 1, :], A[b][l].partition_broadcast(P)),
                     (gain_f[:, 0, :], per_feature(g, l)), (gain_f[:, 1, :], per_feature(b, l)))

            def deviations():
                for t in range(NT):
                    act.wait_ge(s["variance"], t + 1)
                    act.activation(dev[:, t:t + 1], mv[:, t, 1:2], ACT.Sqrt).then_inc(s["deviation"], 1)

            def norm_high_parts():
                high_parts(x_hi, affine=lambda k: (gain_f[:, 0, k:k + 1], gain_f[:, 1, k:k + 1]))

            act.dma_start(const[:, :], A["tables"]).then_inc(start, 16)
            act.dma_start(res[:, :, :], A["x"][0].rearrange("(t p) d -> p t d", p=P)).then_inc(start, 16)
            act.wait_ge(start, 16 * 2)
            split(RING)
            high_parts(x_hi)
            barrier()
            for j in range(8):
                m = 68 if j == 7 else P
                act.wait_ge(s["products"], j + 1)
                act.activation(pf[:m, j, :], ps[:m, j, :], ACT.Copy).then_inc(s["evacuated"], 1)
                if j % 2:
                    split(2)
            barrier()
            act.wait_ge(s["products"], 11)
            tv = ps[:, 2, :].rearrange("p (t n) -> p t n", t=NT)
            act.activation(vt1[:, :, :], tv[:, :, HD:2 * HD], ACT.Copy)
            act.wait_ge(s["products"], 12)
            tw = ps[:, 3, :].rearrange("p (t n) -> p t n", t=NT)
            act.activation(iw[:, :, :], tw[:, :, 64:68], ACT.Copy, scale=IDX_SCALE)
            barrier()
            for i in range(1, NT):
                w = (i + 1) * P
                for h in range(I_HEADS):
                    act.wait_ge(s["scores"], 4 * (i - 1) + h + 1)
                    if i >= 2:
                        act.wait_ge(s["relu_used"], 4 * (i - 2) + h + 1)
                    act.activation(rl[:, h, 0:w], ps[:, h, 0:w], ACT.Relu).then_inc(s["relu"], 1)
            for j in range(6):
                act.wait_ge(s["products"], j + 1)
                act.activation(pf[:, 8 + j, :], ps[:, j, :], ACT.Copy).then_inc(s["evacuated"], 1)
                if j % 2:
                    split(2)
            act.wait_ge(s["dt_products"], 1)
            act.activation(dt_raw[:, :], ps[:, 6, 0:32], ACT.Copy)
            split(4)
            for t in range(NT):
                act.wait_ge(s["products"], 6 + t + 1)
                act.activation(zt[:, t, :], ps[:, t, :], ACT.Silu)
            barrier()
            load((taps[:, :, 0:6], per_feature("conv_w", 0)),
                 (tap_bias[:, 0:6], per_feature("conv_b", 0)),
                 (head_in[:, 0, :], A["dt_bias"][0].partition_broadcast(P)),
                 (head_in[:, 1, :], A["a_log"][0].partition_broadcast(P)),
                 (head_in[:, 2, :], A["d_skip"][0].partition_broadcast(P)),
                 (norm_w[:, :], per_feature("ssd_norm_w", 0)))
            attention(UNITS1, width1, sc1, pt1)
            act.wait_ge(s["params_landed"], 16 * 6)
            split(1)
            barrier()
            for c in range(6):
                act.activation(xc1[:, c, :], pf[:, 8 + c, :], ACT.Identity, scale=taps[:, 3, c:c + 1],
                               bias=tap_bias[:, c:c + 1]).then_inc(s["taps0"], 1)
            act.activation(head_in[:, 3, :], head_in[:, 1, :], ACT.Exp).then_inc(s["gate_exp"], 1)
            softplus(sp[:, 2, :], sp[:, 1, :], sp[:, 4, :], sp[:, 3, :])
            for c in range(6):
                act.wait_ge(s["convolved"], c + 1)
                act.activation(xc1[:, c, :], xc1[:, c, :], ACT.Silu).then_inc(s["activated"], 1)
            for c in range(4):
                act.wait_ge(s["transposed"], c + 1)
                act.activation(xt1[:, :, c * P:c * P + P], ps[:, c, :].rearrange("p (t n) -> p t n", t=NT),
                               ACT.Copy).then_inc(s["tokens_x"], 1)
            act.wait_ge(s["transposed"], 5)
            act.activation(bt1[:, :, :], ps[:, 4, :].rearrange("p (t n) -> p t n", t=NT), ACT.Copy)
            act.wait_ge(s["decay_in"], 1)
            act.activation(dec[:, 4, :], dec[:, 0, :], ACT.Exp).then_inc(s["decays"], 1)
            act.activation(dec[:, 5, :], dec[:, 3, :], ACT.Exp).then_inc(s["decays"], 1)
            act.activation(dec_t[:, :], dec[:, 2, :], ACT.Exp).then_inc(s["decays"], 1)
            barrier()
            for j in range(2 * NT):
                act.wait_ge(s["decay_masked"], j + 1)
                for h in range(4):
                    col = (j // 2) * 8 + (j % 2) * 4 + h
                    act.activation(lm[:, j % 2, h, :], lm[:, j % 2, h, :], ACT.Exp, bias=dec[:, 1, col:col + 1])\
                       .then_inc(s["decay_exp"], 1)
            act.wait_ge(s["variance"], 1)
            act.activation(dev[:, :], mv[:, :, 0], ACT.Sqrt).then_inc(s["deviation"], 1)
            barrier()
            high_parts(oh1, affine=lambda k: (1.0, 0.0) if k < 4 else (norm_w[:, k - 4:k - 3], 0.0))
            barrier()
            load_norm("ln1_g", "ln1_b", 0)
            load((route_b[:, :], A["b_route"][0].partition_broadcast(P)))
            split(7)
            deviations()
            act.wait_ge(s["params_landed"], 16 * 5)
            norm_high_parts()
            barrier()
            act.wait_ge(s["products"], 1)
            act.activation(rt[:, :, 0:20], ps[:, 7, 0:P].rearrange("p (t n) -> p t n", t=NT)[:, :, 0:20], ACT.Copy)\
               .then_inc(s["evacuated"], 1)
            split(N_FIRST + RING - slab.n)
            act.wait_ge(s["gate_in"], 1)
            act.activation(rt[:, :, 24:28], rt[:, :, 24:28], ACT.Exp).then_inc(s["gate_exp"], 1)
            act.wait_ge(s["gate_in"], 2)
            act.activation(rt[:, :, 52:53], rt[:, :, 52:53], ACT.Exp).then_inc(s["gate_exp"], 1)

            def expert(e, after):
                for c in range(2):
                    act.wait_ge(s["gates_full"], 2 * e + (c + 1))
                    act.activation(esg[:, c, :], ps[:, c, :], ACT.Silu).then_inc(s["silu_done"], 1)
                split(3)
                for c in range(2):
                    act.wait_ge(s["hidden"], 2 * e + (c + 1))
                    act.activation(eh[:, c, :], ehd[:, c, :], ACT.Copy).then_inc(s["hidden_hi"], 1)
                split(after)

            with act.Fori(0, EXPERTS - 1) as e:
                slab.enter(e * N_EXPERT, e * (N_EXPERT // RING))
                expert(e, 3)
            slab.leave()
            slab.n += (EXPERTS - 2) * N_EXPERT
            expert(EXPERTS - 1, 0)
            assert slab.n == L_BASE, slab.n
            barrier()
            load_norm("ln2_g", "ln2_b", 0)
            deviations()
            act.wait_ge(s["params_landed"], 16 * 4)
            barrier()

            with act.Fori(0, LAYERS) as l:
                slab.enter(l * N_LAYER, l * (N_LAYER // RING))
                end = slab.n + N_LAYER
                load((taps[:, :, :], per_feature("conv_w_2", l)),
                     (tap_bias[:, :], per_feature("conv_b_2", l)),
                     (gate_bias[:, 0, :], per_feature("b_rg_2", l)),
                     (gate_bias[:, 1, :], per_feature("b_ig_2", l)),
                     (lam[:, 0, :], per_feature("lru_lambda_2", l)),
                     (sink[:, :], A["sinks_2"][l].partition_broadcast(P)))
                split(RING)
                high_parts(x_hi)
                act.wait_ge(s["params_landed"], 16 * 6)
                barrier()
                for j in range(10):
                    act.wait_ge(s["products"], j + 1)
                    dst = qf[:, j, :] if j < 8 else (kr[:, :] if j == 8 else vr[:, :])
                    act.activation(dst, ps[:, j % 8, :], ACT.Copy).then_inc(s["evacuated"], 1)
                    if j % 2:
                        split(2)
                barrier()
                softplus(lam[:, 2, :], lam[:, 1, :], lam[:, 4, :], lam[:, 3, :])
                act.wait_ge(s["products"], 10)
                act.activation(vt2[:, :, :], ps[:, 1, :].rearrange("p (t n) -> p t n", t=NT), ACT.Copy)
                act.wait_ge(s["products"], 11)
                act.activation(ks[:, 1, :], ps[:, 2, :], ACT.Copy)
                barrier()
                attention(UNITS2, width2, sc2, pt2, lambda unit, h: 2 * unit[1] + h)
                barrier()
                high_parts(oh2)
                barrier()

                def gates_of(p):
                    b = 4 * (p % 2)
                    for c in range(2):
                        act.wait_ge(s["products"], 4 * p + c + 1)
                        if p >= 1:
                            act.wait_ge(s["banks_read"], 2 * (p - 1) + c + 1)
                        act.activation(sgm[:, c, :], ps[:, b + c, :], ACT.Sigmoid).then_inc(s["evacuated"], 1)
                    split(2)

                for p in range(4):
                    gates_of(p)
                    split(2)
                barrier()
                for j in range(8):
                    act.wait_ge(s["products"], j + 1)
                    if j >= 4:
                        act.wait_ge(s["convolved"], j - 3)
                    link(act.activation(t4[:, j % 4, :], ps[:, j, :], ACT.Copy))
                    act.activation(xc2[:, j, :], t4[:, j % 4, :], ACT.Identity, scale=taps[:, 3, j:j + 1],
                                   bias=tap_bias[:, j:j + 1]).then_inc(s["taps0"], 1)
                    if j % 2:
                        split(2)
                        for i in ((j - 3, j - 2) if j >= 3 else ()):
                            act.wait_ge(s["convolved"], i + 1)
                            act.activation(yh[:, i, :], xc2[:, i, :], ACT.Copy).then_inc(s["hi_ready"], 1)
                for i in (6, 7):
                    act.wait_ge(s["convolved"], i + 1)
                    act.activation(yh[:, i, :], xc2[:, i, :], ACT.Copy).then_inc(s["hi_ready"], 1)
                barrier()
                for j in range(8):
                    act.wait_ge(s["products"], j + 1)
                    act.activation(ga[:, j, :], ps[:, j, :], ACT.Sigmoid, bias=gate_bias[:, 0, j:j + 1])\
                       .then_inc(s["r_done"], 1)
                    if j % 4 == 3:
                        split(1)
                for j in range(8):
                    act.wait_ge(s["products"], 8 + j + 1)
                    if j >= 2:
                        act.wait_ge(s["i_used"], j - 1)
                    act.activation(vbuf[:, j % 2, :], ps[:, j, :], ACT.Sigmoid, bias=gate_bias[:, 1, j:j + 1])\
                       .then_inc(s["i_done"], 1)
                    if j % 4 == 3:
                        split(1)
                for j in range(8):
                    act.activation(t8[:, j, :], ga[:, j, :], ACT.Tanh, scale=lam[:, 6, j:j + 1])\
                       .then_inc(s["tanh_done"], 1)
                for j in range(8):
                    act.activation(ga[:, j, :], ga[:, j, :], ACT.Exp, scale=lam[:, 7, j:j + 1])\
                       .then_inc(s["decay_done"], 1)
                for j in range(8):
                    act.wait_ge(s["mult2"], j + 1)
                    act.activation(t8[:, j, :], t8[:, j, :], ACT.Sqrt).then_inc(s["mult"], 1)
                barrier()
                for j in range(8):
                    act.wait_ge(s["products"], j + 1)
                    if j >= 4:
                        act.wait_ge(s["chunk_ready"], j - 3)
                    act.activation(t4[:, j % 4, :], ps[:, j, :], ACT.Gelu_apprx_tanh).then_inc(s["gelu_done"], 1)
                    if j % 2:
                        split(2)
                        for i in (j - 1, j):
                            act.wait_ge(s["chunk_ready"], i + 1)
                            act.activation(yh[:, i, :], xc2[:, i, :], ACT.Copy).then_inc(s["hi_ready"], 1)
                barrier()
                for p in range(4):
                    gates_of(p)
                    for j in (2 * p, 2 * p + 1):
                        act.wait_ge(s["chunk_ready"], j + 1)
                        act.activation(mh[:, j, :], mg[:, j, :], ACT.Copy).then_inc(s["hi_ready"], 1)
                    split(2)
                barrier()
                load_norm("ln1_g_2", "ln1_b_2", l)
                split(8)
                deviations()
                act.wait_ge(s["params_landed"], 16 * 4)
                norm_high_parts()
                barrier()
                load((mt[:, :, :], A["mem_2"][0].rearrange("(t p) d -> p t d", p=P)))
                high_parts(mem_h, nt=MEM)
                barrier()
                for j in range(8):
                    act.wait_ge(s["products"], j + 1)
                    act.activation(kc[:, j, :], ps[:, j, 0:MEM], ACT.Copy).then_inc(s["evacuated"], 1)
                    if j % 2:
                        split(2)
                split(8)
                for t in range(2):
                    act.wait_ge(s["products"], 8 + t + 1)
                    act.activation(vc[:, t, :].rearrange("p (h n) -> p h n", h=2), ps[:, 2 * t:2 * t + 2, :], ACT.Copy)
                barrier()
                for j in range(8):
                    act.wait_ge(s["products"], j + 1)
                    act.activation(qc[:, j, :], ps[:, j, :], ACT.Copy)
                    if j % 2:
                        split(2)
                barrier()
                attention(UNITS3, width3, sc3, pt3)
                barrier()
                high_parts(oh3)
                barrier()
                load_norm("ln2_g_2", "ln2_b_2", l)
                split(8)
                deviations()
                act.wait_ge(s["params_landed"], 16 * 4)
                norm_high_parts()
                barrier()
                for half, (c0, n) in enumerate(FF_HALVES):
                    for p in range(n // 2):
                        b = 4 * (p % 2)
                        for c in range(2):
                            act.wait_ge(s["gates_full"], 2 * p + c + 1)
                            if p >= 2:
                                act.wait_ge(s["hidden"], 2 * (p - 2) + c + 1)
                            act.activation(fsg[:, p % 2, c, :], ps[:, b + c, :], ACT.Silu).then_inc(s["silu_done"], 1)
                        split(2, end)
                        for c in range(2):
                            act.wait_ge(s["hidden"], 2 * p + c + 1)
                            act.activation(fh[:, 2 * p + c, :], fhd[:, c, :], ACT.Copy).then_inc(s["hidden_hi"], 1)
                        split(2, end)
                    split(n, end)
                    barrier()
                load_norm("ln3_g_2", "ln3_b_2", l)
                deviations()
                act.wait_ge(s["params_landed"], 16 * 4)
                barrier()
                assert slab.n == end

        @block.vector
        def _(dve):
            phase = Count()
            links = [0]

            def link(ins):
                links[0] += 1
                ins.then_inc(s["dve_link"], 1)
                dve.wait_ge(s["dve_link"], links[0])

            def barrier():
                dve.wait_ge(arrived, 2)
                dve.drain()
                dve.sem_clear(phase_range)
                dve.sem_clear(arrived)
                dve.sem_clear(go[1 - phase.n % 2])
                dve.drain().then_inc(go[phase.n % 2], 1)
                phase.n += 1
                links[0] = 0

            def low_parts(hi, lo, source, nt=T, count=KD):
                for k in range(count):
                    dve.wait_ge(s["hi_ready"], k + 1)
                    dve.tensor_tensor(lo[:, k, 0:nt], source(k), hi[:, k, 0:nt].bitcast(F32), ALU.subtract)\
                       .then_inc(s["lo_ready"], 1)

            def from_banks(nt=T):
                return lambda k: ps[:, k, 0:nt]

            def from_vbuf(k):
                return vbuf[:, k % 2, :]

            def heads(v, n):
                return v.rearrange("p (h n) -> p h n", h=n)

            def wide(v, n):
                return v.unsqueeze(2).broadcast_to([v.shape[0], v.shape[1], n])

            def attention(units, width, sc, mask_of, scale, out_of, sinks=None):
                def finish(u):
                    dst = out_of(units[u])
                    dv = dst.shape[2]
                    dve.wait_ge(s["values"], u + 1)
                    if sinks:
                        dve.wait_ge(s["sink_exp"], 2 * u + 2)
                        link(dve.tensor_tensor(den[:, u % 2, :], den[:, u % 2, :], esink[:, u % 2, :], ALU.add))
                    link(dve.reciprocal(rden[:, u % 2, :], den[:, u % 2, :]))
                    dve.tensor_tensor(dst, heads(ps[:, 6 + u % 2, 0:2 * dv], 2), wide(rden[:, u % 2, :], dv), ALU.mult)\
                       .then_inc(s["values_read"], 1)

                for u, unit in enumerate(units):
                    w = width(unit)
                    dve.wait_ge(s["scores"], u + 1)
                    if u >= 2:
                        dve.wait_ge(s["probs_t"], u - 1)
                    dst, src = sc[:, u % 2, :, 0:w], ps[:, 2 * (u % 2):2 * (u % 2) + 2, 0:w]
                    mask = mask_of(unit)
                    if mask is None:
                        dve.tensor_scalar(dst, src, scale, None, ALU.mult).then_inc(s["scores_read"], 1)
                    else:
                        dve.scalar_tensor_tensor(dst, src, scale, mask.unsqueeze(1).broadcast_to([P, 2, w]),
                                                 ALU.mult, ALU.add).then_inc(s["scores_read"], 1)
                    dve.wait_ge(s["scores_read"], u + 1)
                    if sinks:
                        link(dve.tensor_reduce(nmax[:, u % 2, :], dst, AX.X, ALU.max))
                        link(dve.tensor_tensor(nmax[:, u % 2, :], nmax[:, u % 2, :], sinks(unit), ALU.max))
                        dve.tensor_scalar(nmax[:, u % 2, :], nmax[:, u % 2, :], -1.0, None, ALU.mult)\
                           .then_inc(s["maxima"], 1)
                    else:
                        dve.tensor_reduce(nmax[:, u % 2, :], dst, AX.X, ALU.max, negate=True).then_inc(s["maxima"], 1)
                    if u >= 1:
                        finish(u - 1)
                finish(len(units) - 1)

            def softplus_start(x, mag):
                link(dve.tensor_scalar(mag, x, -1.0, None, ALU.mult))
                dve.tensor_tensor(mag, mag, x, ALU.max).then_inc(s["sp_in"], 1)

            def softplus_end(x, e, u, log, tmp, to):
                dve.wait_ge(s["sp_exp"], 1)
                dve.tensor_scalar(u, e, 1.0, None, ALU.add).then_inc(s["sp_sum"], 1)
                dve.wait_ge(s["sp_sum"], 1)
                link(dve.tensor_scalar(tmp, u, -1.0, None, ALU.add))
                link(dve.tensor_tensor(tmp, e, tmp, ALU.subtract))
                link(dve.reciprocal(to, u))
                link(dve.tensor_tensor(tmp, tmp, to, ALU.mult))
                dve.wait_ge(s["sp_log"], 1)
                link(dve.tensor_tensor(tmp, tmp, log, ALU.add))
                link(dve.tensor_scalar(to, x, 0.0, None, ALU.max))
                link(dve.tensor_tensor(to, to, tmp, ALU.add))

            def layer_norm(alpha, in_banks=True):
                def first(t):
                    if in_banks:
                        dve.wait_ge(s["products"], t + 1)
                        y = res[:, t, :].rearrange("p (a b) -> p a b", a=2)
                        dve.scalar_tensor_tensor(y, y, alpha, ps[:, 2 * t:2 * t + 2, :], ALU.mult, ALU.add)\
                           .then_inc(s["summed"], 1)
                        dve.wait_ge(s["summed"], t + 1)
                    dve.bn_stats(stats[:, t, 0, :], res[:, t, 0:512])
                    link(dve.bn_stats(stats[:, t, 1, :], res[:, t, 512:D]))
                    link(dve.bn_aggr(mv[:, t, :], stats[:, t, :, :]))
                    dve.tensor_scalar(mv[:, t, 1:2], mv[:, t, 1:2], EPS, None, ALU.add).then_inc(s["variance"], 1)

                def second(t):
                    dve.wait_ge(s["deviation"], t + 1)
                    link(dve.reciprocal(rdev[:, t:t + 1], dev[:, t:t + 1]))
                    dve.tensor_scalar(res[:, t, :], res[:, t, :], mv[:, t, 0:1], rdev[:, t:t + 1],
                                      ALU.subtract, ALU.mult).then_inc(s["normalised"], 1)

                first(0)
                for t in range(1, NT):
                    first(t)
                    second(t - 1)
                second(NT - 1)

            def residual_gain(scale=None):
                for t in range(NT):
                    ins = dve.tensor_tensor(res[:, t, :], res[:, t, :], gain[:, 0, :], ALU.mult)
                link(ins)
                for t in range(NT):
                    ins = dve.tensor_tensor(res[:, t, :], res[:, t, :], gain[:, 1, :], ALU.add)
                link(ins)
                if scale is not None:
                    link(dve.tensor_scalar(res[:, :, :], res[:, :, :], scale, None, ALU.mult))

            low_parts(x_hi, x_lo, from_banks())
            barrier()
            barrier()
            cos, sin = consts["cos1"], consts["sin1"]
            for j, c in enumerate((0, 1, 2, 3, 5, 6)):
                dve.wait_ge(s["products"], j + 1)
                dve.tensor_tensor(rl[:, 0, :], ps[:, j, :], sin, ALU.mult).then_inc(s["banks_read"], 1)
                link(dve.tensor_tensor(rl[:, 1, :], pf[:, c, :], cos, ALU.mult))
                dve.wait_ge(s["banks_read"], j + 1)
                link(dve.tensor_tensor(pf[:, c, :], rl[:, 0, :], rl[:, 1, :], ALU.add))
            for c, plain, turned, ready in ((4, 6, 7, 11), (7, 0, 1, 12)):
                dve.wait_ge(s["products"], ready)
                link(dve.tensor_tensor(rl[:, 0, :], ps[:, turned, :], sin, ALU.mult))
                link(dve.tensor_tensor(rl[:, 1, :], ps[:, plain, :], cos, ALU.mult))
                link(dve.tensor_tensor(pf[:, c, :], rl[:, 0, :], rl[:, 1, :], ALU.add))
            barrier()
            link(dve.memset(ones[:, :], 1.0))
            for i in range(1, NT):
                w = (i + 1) * P
                for h in range(I_HEADS):
                    n = 4 * (i - 1) + h + 1
                    dve.wait_ge(s["relu"], n)
                    if h == 0:
                        dve.tensor_scalar(ix[:, i - 1, 0:w], rl[:, h, 0:w], iw[:, i, h:h + 1], None, ALU.mult)\
                           .then_inc(s["relu_used"], 1)
                    else:
                        dve.scalar_tensor_tensor(ix[:, i - 1, 0:w], rl[:, h, 0:w], iw[:, i, h:h + 1],
                                                 ix[:, i - 1, 0:w], ALU.mult, ALU.add).then_inc(s["relu_used"], 1)
                    dve.wait_ge(s["relu_used"], n)
                link(dve.tensor_tensor(ix[:, i - 1, w - P:w], ix[:, i - 1, w - P:w], consts["cmask"], ALU.add))
            link(dve.tensor_copy(mb[:, 0, 0:P], consts["cmask"]))
            for i in range(1, NT):
                w = (i + 1) * P
                sc, work, eq, pre = ix[:, i - 1, 0:w], ix[:, 3, 0:w], rl[:, 0, 0:w], rl[:, 1, 0:w]
                for r in range(TOPK // 8):
                    link(dve.max(top8[:, :], sc if r == 0 else work))
                    if r < TOPK // 8 - 1:
                        link(dve.match_replace(work, top8[:, :], sc if r == 0 else work, GONE))
                least = top8[:, 7:8]
                link(dve.tensor_scalar(mb[:, i, 0:w], sc, least, None, ALU.is_gt))
                link(dve.tensor_reduce(short[:, :], mb[:, i, 0:w], AX.X, ALU.add))
                link(dve.tensor_scalar(short[:, :], short[:, :], -1.0, float(TOPK), ALU.mult, ALU.add))
                link(dve.tensor_scalar(eq, sc, least, None, ALU.is_equal))
                link(dve.tensor_tensor_scan(pre, ones[:, 0:w], eq, 0.0, ALU.mult, ALU.add))
                link(dve.scalar_tensor_tensor(eq, pre, short[:, 0:1], eq, ALU.is_le, ALU.mult))
                link(dve.tensor_tensor(mb[:, i, 0:w], mb[:, i, 0:w], eq, ALU.add))
                link(dve.tensor_scalar(mb[:, i, 0:w], mb[:, i, 0:w], -1.0, -NEG, ALU.add, ALU.mult))
            barrier()
            attention(UNITS1, width1, sc1, lambda unit: mb[:, unit[0], 0:width1(unit)], HD ** -0.5,
                      lambda unit: heads(ot1[:, unit[0], P * unit[1]:P * unit[1] + P], 2))
            barrier()
            x_sp, mag, e_sp, u_sp, l_sp, tmp, dt = (sp[:, i, :] for i in range(7))
            link(dve.tensor_tensor(x_sp.rearrange("p (t h) -> p t h", t=NT), dt_raw[:, :].rearrange("p (t h) -> p t h", t=NT),
                                   head_in[:, 0:1, :].broadcast_to([P, NT, 8]), ALU.add))
            softplus_start(x_sp, mag)
            for c in range(6):
                dve.wait_ge(s["taps0"], c + 1)
                for back in (1, 2, 3):
                    ins = dve.scalar_tensor_tensor(xc1[:, c, back:T], pf[:, 8 + c, 0:T - back], taps[:, 3 - back, c:c + 1],
                                                   xc1[:, c, back:T], ALU.mult, ALU.add)
                    if back < 3:
                        link(ins)
                ins.then_inc(s["convolved"], 1)
            softplus_end(x_sp, e_sp, u_sp, l_sp, tmp, dt)
            dve.wait_ge(s["gate_exp"], 1)
            link(dve.tensor_tensor(dt_a[:, :].rearrange("p (t h) -> p t h", t=NT), dt.rearrange("p (t h) -> p t h", t=NT),
                                   head_in[:, 3:4, :].broadcast_to([P, NT, 8]), ALU.mult))
            dve.tensor_scalar(dt_a[:, :], dt_a[:, :], -1.0, None, ALU.mult).then_inc(s["sp_done"], 1)
            dve.wait_ge(s["cumulated"], 1)
            link(dve.tensor_copy(dec[:, 0, :], ps[:, 5, 0:32]))
            link(dve.tensor_copy(dec[:, 2, :], ps[:, 6, 0:32]))
            link(dve.tensor_scalar(dec[:, 1, :], dec[:, 0, :], -1.0, None, ALU.mult))
            dve.tensor_tensor(dec[:, 3, :], dec[:, 2, :], dec[:, 0, :], ALU.subtract).then_inc(s["decay_in"], 1)
            dve.wait_ge(s["tokens_x"], 4)
            x3, xdt3, xdec3 = (v[:, :, :].rearrange("p t (h n) -> p (t h) n", n=HD) for v in (xt1, xdt, xdec))
            link(dve.tensor_tensor(xdt3, x3, wide(dt, HD), ALU.mult))
            for t in range(NT):
                dve.tensor_tensor(heads(xsk[:, t, :], 8), heads(xt1[:, t, :], 8), wide(head_in[:, 2, :], HD), ALU.mult)
            dve.wait_ge(s["decays"], 3)
            dve.tensor_tensor(xdec3, xdt3, wide(dec[:, 5, :], HD), ALU.mult)
            dve.memset(prev[:, :], 0.0)
            dt3 = dec_t[:, :].rearrange("p (t h) -> p t h", t=NT)
            for g in range(S_GROUPS):
                r = slice(HD * g, HD * g + HD)
                dve.tensor_copy(dec4[r, :, :], dt3[r, :, 4 * g:4 * g + 4])
            barrier()
            for c in range(NT):
                for g in range(S_GROUPS):
                    j = 2 * c + g
                    dve.wait_ge(s["cb_products"], j + 1)
                    if c >= 1 and g == 0:
                        dve.wait_ge(s["chunk_products"], c)
                    dve.tensor_tensor(lm[:, g, :, :], heads(ps[:, 2 + g, :], 4),
                                      consts["cmask_t"].unsqueeze(1).broadcast_to([P, 4, P]), ALU.add)\
                       .then_inc(s["decay_masked"], 1)
                for g in range(S_GROUPS):
                    j = 2 * c + g
                    dve.wait_ge(s["decay_exp"], 4 * (j + 1))
                    dve.tensor_tensor(lm[:, g, :, :], lm[:, g, :, :],
                                      ps[:, g, 0:P].unsqueeze(1).broadcast_to([P, 4, P]), ALU.mult)\
                       .then_inc(s["decayed"], 1)
                dve.wait_ge(s["chunk_products"], c + 1)
                for g in range(S_GROUPS):
                    ins = dve.tensor_tensor(heads(yt[:, 256 * g:256 * g + 256], 4), heads(ps[:, 5 + 2 * g, 0:256], 4),
                                            wide(dec[:, 4, 8 * c + 4 * g:8 * c + 4 * g + 4], HD), ALU.mult)
                link(ins)
                link(dve.tensor_tensor(yt[:, :], yt[:, :], ps[:, 4, :], ALU.add))
                link(dve.tensor_tensor(heads(prev[:, :], 4), heads(prev[:, :], 4), wide(dec4[:, c, :], HD), ALU.mult))
                dve.tensor_tensor(prev[:, :], prev[:, :], ps[:, 6, 0:256], ALU.add).then_inc(s["state_ready"], 1)
                dve.wait_ge(s["state_ready"], c + 1)
                link(dve.tensor_tensor(yt[:, :], yt[:, :], xsk[:, c, :], ALU.add))
                link(dve.tensor_tensor(ot1[:, c, 512:D], yt[:, :], zt[:, c, :], ALU.mult))
                link(dve.scalar_tensor_tensor(sq[:, :], ot1[:, c, 512:D], 1.0, ot1[:, c, 512:D], ALU.mult, ALU.mult,
                                              accum_out=mv[:, c, 0:1]))
            dve.tensor_scalar(mv[:, :, 0], mv[:, :, 0], 1.0 / 512, EPS, ALU.mult, ALU.add).then_inc(s["variance"], 1)
            dve.wait_ge(s["deviation"], 1)
            link(dve.reciprocal(rdev[:, :], dev[:, :]))
            for c in range(NT):
                dve.tensor_scalar(ot1[:, c, 512:D], ot1[:, c, 512:D], rdev[:, c:c + 1], None, ALU.mult)
            barrier()
            low_parts(oh1, ol1, from_vbuf)
            barrier()
            layer_norm(ALPHA1)
            low_parts(x_hi, x_lo, from_vbuf)
            barrier()
            residual_gain(ALPHA1)
            dve.wait_ge(s["evacuated"], 1)
            link(dve.tensor_tensor(rt[:, :, 0:20], rt[:, :, 0:20],
                                   route_b[:, :].unsqueeze(1).broadcast_to([P, NT, 20]), ALU.add))
            one4 = lambda v, n: v.broadcast_to([P, NT, n])

            def first_of_best(logits, best, onehot):
                link(dve.tensor_reduce(best, logits, AX.X, ALU.max))
                link(dve.tensor_tensor(onehot, logits, one4(best, 4), ALU.is_equal))
                link(dve.tensor_tensor(onehot, onehot, rank, ALU.mult))
                link(dve.tensor_reduce(rt[:, :, 63:64], onehot, AX.X, ALU.max))
                link(dve.tensor_tensor(onehot, rank, one4(rt[:, :, 63:64], 4), ALU.is_equal))

            rank = rt[:, :, 56:60]
            for j in range(4):
                link(dve.memset(rt[:, :, 56 + j:57 + j], float(4 - j)))
            g_log, g_max, g_hot, g_exp = rt[:, :, 0:4], rt[:, :, 20:21], rt[:, :, 28:32], rt[:, :, 24:28]
            first_of_best(g_log, g_max, g_hot)
            dve.tensor_tensor(g_exp, g_log, one4(g_max, 4), ALU.subtract).then_inc(s["gate_in"], 1)
            e_log, e_tmp = rt[:, :, 32:36], rt[:, :, 36:40]
            link(dve.tensor_tensor(e_log, rt[:, :, 4:8], one4(rt[:, :, 28:29], 4), ALU.mult))
            for g in range(1, GROUPS):
                link(dve.tensor_tensor(e_tmp, rt[:, :, 4 + 4 * g:8 + 4 * g], one4(rt[:, :, 28 + g:29 + g], 4), ALU.mult))
                link(dve.tensor_tensor(e_log, e_log, e_tmp, ALU.add))
            m1, m2, hot1, hot2, e12 = rt[:, :, 21:22], rt[:, :, 22:23], rt[:, :, 40:44], rt[:, :, 44:48], rt[:, :, 52:53]
            first_of_best(e_log, m1, hot1)
            link(dve.tensor_scalar(e_tmp, hot1, NEG, None, ALU.mult))
            link(dve.tensor_tensor(e_tmp, e_tmp, e_log, ALU.add))
            first_of_best(e_tmp, m2, hot2)
            dve.tensor_tensor(e12, m2, m1, ALU.subtract).then_inc(s["gate_in"], 1)
            dve.wait_ge(s["gate_exp"], 2)
            gsum, w1, w2 = rt[:, :, 53:54], rt[:, :, 54:55], rt[:, :, 55:56]
            link(dve.tensor_reduce(gsum, g_exp, AX.X, ALU.add))
            link(dve.tensor_scalar(w1, e12, 1.0, None, ALU.add))
            link(dve.tensor_tensor(w1, w1, gsum, ALU.mult))
            link(dve.reciprocal(w1, w1))
            link(dve.tensor_tensor(w2, w1, e12, ALU.mult))
            link(dve.tensor_tensor(hot1, hot1, one4(w1, 4), ALU.mult))
            link(dve.tensor_tensor(hot2, hot2, one4(w2, 4), ALU.mult))
            link(dve.tensor_tensor(hot1, hot1, hot2, ALU.add))
            for g in range(GROUPS):
                link(dve.tensor_tensor(gates[:, :, 4 * g:4 * g + 4], hot1, one4(rt[:, :, 28 + g:29 + g], 4), ALU.mult))

            def expert_hidden(e):
                for c in range(2):
                    dve.wait_ge(s["silu_done"], 2 * e + (c + 1))
                    dve.wait_ge(s["ups_full"], 2 * e + (c + 1))
                    dve.tensor_tensor(ehd[:, c, :], esg[:, c, :], ps[:, 2 + c, :], ALU.mult).then_inc(s["hidden"], 1)
                for c in range(2):
                    dve.wait_ge(s["hidden_hi"], 2 * e + (c + 1))
                    dve.tensor_tensor(el[:, c, :], ehd[:, c, :], eh[:, c, :].bitcast(F32), ALU.subtract)\
                       .then_inc(s["hidden_lo"], 1)

            def expert_sum(e):
                for half in range(2):
                    for t in range(NT):
                        dve.wait_ge(s["downs_full"], 8 * e + (4 * half + t + 1))
                        y = res[:, t, 512 * half:512 * half + 512]
                        gate = gates[:, t, bass.ds(e, 1)]
                        dve.scalar_tensor_tensor(y, ps[:, 4 + t, :], gate, y, ALU.mult, ALU.add)\
                           .then_inc(s["downs_free"], 1)

            expert_hidden(0)
            with dve.Fori(0, EXPERTS - 1) as e:
                expert_sum(e)
                expert_hidden(e + 1)
            expert_sum(EXPERTS - 1)
            barrier()
            layer_norm(1.0, in_banks=False)
            dve.wait_ge(s["params_landed"], 16 * 4)
            dve.wait_ge(s["normalised"], NT)
            residual_gain()
            barrier()

            with dve.Fori(0, LAYERS) as l:
                low_parts(x_hi, x_lo, from_banks())
                barrier()
                barrier()
                link(dve.tensor_scalar(lam[:, 0, :], lam[:, 0, :], -1.0, None, ALU.mult))
                softplus_start(lam[:, 0, :], lam[:, 1, :])
                softplus_end(lam[:, 0, :], lam[:, 2, :], lam[:, 3, :], lam[:, 4, :], lam[:, 5, :], lam[:, 6, :])
                link(dve.tensor_scalar(lam[:, 7, :], lam[:, 6, :], -8.0, None, ALU.mult))
                link(dve.tensor_scalar(lam[:, 6, :], lam[:, 6, :], 8.0, None, ALU.mult))
                for j in range(9):
                    raw, dst = (qf[:, j, :], qf[:, j, :]) if j < 8 else (kr[:, :], ks[:, 0, :])
                    dve.wait_ge(s["products"], j + 1)
                    dve.tensor_tensor(vbuf[:, 0, :], ps[:, j % 8, :], consts["sin2"], ALU.mult)\
                       .then_inc(s["banks_read"], 1)
                    link(dve.tensor_tensor(vbuf[:, 1, :], raw, consts["cos2"], ALU.mult))
                    dve.wait_ge(s["banks_read"], j + 1)
                    dve.tensor_tensor(dst, vbuf[:, 0, :], vbuf[:, 1, :], ALU.add).then_inc(s["turned"], 1)
                    dve.wait_ge(s["turned"], j + 1)
                barrier()

                def mask2(unit):
                    return consts["swamask"] if unit[0] else consts["swamask"][:, P:2 * P]

                attention(UNITS2, width2, sc2, mask2, HD ** -0.5,
                          lambda unit: heads(ot2[:, unit[0], P * unit[1]:P * unit[1] + P], 2),
                          lambda unit: sink[:, 2 * unit[1]:2 * unit[1] + 2])
                barrier()
                low_parts(oh2, ol2, from_banks())
                barrier()
                for p in range(4):
                    b = 4 * (p % 2)
                    for c in range(2):
                        dve.wait_ge(s["evacuated"], 2 * p + c + 1)
                        dve.wait_ge(s["products"], 4 * p + 2 + c + 1)
                        dve.tensor_tensor(mg[:, 2 * p + c, :], sgm[:, c, :], ps[:, b + 2 + c, :], ALU.mult)\
                           .then_inc(s["banks_read"], 1)
                barrier()
                for j in range(8):
                    dve.wait_ge(s["taps0"], j + 1)
                    for back in (1, 2, 3):
                        ins = dve.scalar_tensor_tensor(xc2[:, j, back:T], t4[:, j % 4, 0:T - back],
                                                       taps[:, 3 - back, j:j + 1], xc2[:, j, back:T], ALU.mult, ALU.add)
                        if back < 3:
                            link(ins)
                    ins.then_inc(s["convolved"], 1)
                low_parts(yh, yl, lambda k: xc2[:, k, :])
                barrier()
                for j in range(8):
                    dve.wait_ge(s["i_done"], j + 1)
                    dve.tensor_tensor(xc2[:, j, :], xc2[:, j, :], vbuf[:, j % 2, :], ALU.mult).then_inc(s["i_used"], 1)
                dve.wait_ge(s["i_used"], 8)
                for j in range(8):
                    dve.wait_ge(s["tanh_done"], j + 1)
                    link(dve.tensor_scalar(vbuf[:, 0, :], t8[:, j, :], 1.0, None, ALU.add))
                    link(dve.reciprocal(vbuf[:, 1, :], vbuf[:, 0, :]))
                    dve.scalar_tensor_tensor(t8[:, j, :], t8[:, j, :], 2.0, vbuf[:, 1, :], ALU.mult, ALU.mult)\
                       .then_inc(s["mult2"], 1)
                    dve.wait_ge(s["mult2"], j + 1)
                for j in range(8):
                    dve.wait_ge(s["mult"], j + 1)
                    link(dve.tensor_tensor(xc2[:, j, :], xc2[:, j, :], t8[:, j, :], ALU.mult))
                    dve.wait_ge(s["decay_done"], j + 1)
                    link(dve.tensor_tensor_scan(t8[:, j, :], ga[:, j, :], xc2[:, j, :], 0.0, ALU.mult, ALU.add))
                    link(dve.tensor_copy(xc2[:, j, :], t8[:, j, :]))
                barrier()
                for j in range(8):
                    dve.wait_ge(s["gelu_done"], j + 1)
                    dve.tensor_tensor(xc2[:, j, :], xc2[:, j, :], t4[:, j % 4, :], ALU.mult).then_inc(s["chunk_ready"], 1)
                    if j % 2:
                        for i in (j - 1, j):
                            dve.wait_ge(s["hi_ready"], i + 1)
                            dve.tensor_tensor(yl[:, i, :], xc2[:, i, :], yh[:, i, :].bitcast(F32), ALU.subtract)
                barrier()
                for p in range(4):
                    b = 4 * (p % 2)
                    for c in range(2):
                        j = 2 * p + c
                        dve.wait_ge(s["evacuated"], j + 1)
                        dve.wait_ge(s["products"], 4 * p + 2 + c + 1)
                        dve.tensor_tensor(vbuf[:, c, :], sgm[:, c, :], ps[:, b + 2 + c, :], ALU.mult)\
                           .then_inc(s["banks_read"], 1)
                        dve.wait_ge(s["banks_read"], j + 1)
                        dve.tensor_tensor(mg[:, j, :], mg[:, j, :], vbuf[:, c, :], ALU.add).then_inc(s["chunk_ready"], 1)
                    for j in (2 * p, 2 * p + 1):
                        dve.wait_ge(s["hi_ready"], j + 1)
                        dve.tensor_tensor(ml[:, j, :], mg[:, j, :], mh[:, j, :].bitcast(F32), ALU.subtract)
                barrier()
                layer_norm(ALPHA2)
                low_parts(x_hi, x_lo, from_vbuf)
                barrier()
                low_parts(mem_h, mem_l, from_banks(MEM), nt=MEM)
                residual_gain()
                barrier()
                barrier()
                barrier()
                attention(UNITS3, width3, sc3, lambda unit: None, 256 ** -0.5,
                          lambda unit: heads(ot3[:, unit[0], 512 * unit[1]:512 * unit[1] + 512], 2))
                barrier()
                low_parts(oh3, ol3, from_banks())
                barrier()
                layer_norm(ALPHA2)
                low_parts(x_hi, x_lo, from_vbuf)
                barrier()
                for half, (c0, n) in enumerate(FF_HALVES):
                    if half == 0:
                        residual_gain()
                    for p in range(n // 2):
                        b = 4 * (p % 2)
                        for c in range(2):
                            j = 2 * p + c
                            dve.wait_ge(s["silu_done"], j + 1)
                            dve.wait_ge(s["ups_full"], j + 1)
                            if p >= 1:
                                dve.wait_ge(s["hidden_hi"], j - 1)
                                dve.wait_ge(s["hidden_lo"], j - 1)
                            dve.tensor_tensor(fhd[:, c, :], fsg[:, p % 2, c, :], ps[:, b + 2 + c, :], ALU.mult)\
                               .then_inc(s["hidden"], 1)
                        for c in range(2):
                            j = 2 * p + c
                            dve.wait_ge(s["hidden_hi"], j + 1)
                            dve.tensor_tensor(fl[:, j, :], fhd[:, c, :], fh[:, j, :].bitcast(F32), ALU.subtract)\
                               .then_inc(s["hidden_lo"], 1)
                    if half == 0:
                        for t in range(NT):
                            dve.wait_ge(s["products"], t + 1)
                            y = res[:, t, :].rearrange("p (a b) -> p a b", a=2)
                            dve.scalar_tensor_tensor(y, y, ALPHA2, ps[:, 2 * t:2 * t + 2, :], ALU.mult, ALU.add)
                    else:
                        for t in range(NT):
                            dve.wait_ge(s["products"], t + 1)
                            y = res[:, t, :].rearrange("p (a b) -> p a b", a=2)
                            dve.tensor_tensor(y, y, ps[:, 2 * t:2 * t + 2, :], ALU.add)
                    barrier()
                layer_norm(1.0, in_banks=False)
                dve.wait_ge(s["params_landed"], 16 * 4)
                dve.wait_ge(s["normalised"], NT)
                residual_gain()
                barrier()
            dve.drain().then_inc(finished, 1)


_PLAIN = ["x", "w_in", "dt_bias", "a_log", "d_skip", "w_out", "ln1_g", "ln1_b",
          "w_gate", "w_up", "w_down", "ln2_g", "ln2_b", "mem_2", "w_in_2", "w_rg_2", 
          "w_ig_2", "w_br_rnn_2", "w_br_attn_2", "sinks_2", "w_out_2", "ln1_g_2", "ln1_b_2",
          "cq_w_2", "ckv_w_2", "co_w_2", "ln2_g_2", "ln2_b_2", "ffn_wi_2", "ffn_wo_2", "ln3_g_2", "ln3_b_2"]


_PER_FEATURE = ["conv_w", "conv_b", "ssd_norm_w", "ln1_g", "ln1_b", "ln2_g", "ln2_b", "conv_w_2", "conv_b_2", "b_rg_2",
                "b_ig_2", "lru_lambda_2", "ln1_g_2", "ln1_b_2", "ln2_g_2", "ln2_b_2", "ln3_g_2", "ln3_b_2"]


def kernel(**inputs):
    import concourse.bacc as bacc
    from concourse.bass_utils import run_bass_kernel_spmd

    data = {name: np.ascontiguousarray(inputs[name]) for name in _PLAIN}
    for name in _PER_FEATURE:
        a = inputs[name]
        a = np.moveaxis(np.asarray(a).reshape(*a.shape[:-1], -1, P), -1, 1)
        data[name + "_f"] = np.ascontiguousarray(a)
    data["w_route"] = np.concatenate([inputs["w_route_group"], inputs["w_route_expert"]], axis=-1)
    data["b_route"] = np.concatenate([inputs["b_route_group"], inputs["b_route_expert"]], axis=-1)
    data["tables"] = tables()
    nc = bacc.Bacc("TRN2", target_bir_lowering=False, num_devices=1)
    arrays, aps = {}, {}
    for name, a in data.items():
        arrays[f"in_{name}"] = a
        aps[name] = nc.dram_tensor(f"in_{name}", a.shape, mybir.dt.from_np(a.dtype), kind="ExternalInput").ap()
    out = nc.dram_tensor("out_0", (1, T, D), F32, kind="ExternalOutput").ap()
    build(nc, aps, out)
    r = run_bass_kernel_spmd(nc, [arrays], core_ids=[0])
    return r.results[0]["out_0"]
```

```python
from contextlib import ExitStack

import numpy as np
import concourse.bass as bass
from concourse import mybir

ALU = mybir.AluOpType
ACT = mybir.ActivationFunctionType
F32 = mybir.dt.float32
F32R = mybir.dt.float32r
AX = mybir.AxisListType

P = 128
T = 512
NT = T // P
D = 1024
KD = D // P
HD = 64
NEG = -1.0e30
GONE = -3.0e38
EPS = 1e-5

A_HEADS, I_HEADS, TOPK = 8, 4, 128
S_HEADS, S_GROUPS = 8, 2
EXPERTS, GROUPS, FF1 = 16, 4, 256
ALPHA1 = 2 ** 0.25
IDX_SCALE = (I_HEADS ** -0.5) * (HD ** -0.5)
Q0, KV0, IQ0, IK0, Z0, XBC0, DT0 = 0, 512, 640, 896, 964, 1476, 2244
LAYERS, MEM = 2, 256
ALPHA2 = 4 ** 0.25
Q_HEADS2, KV_HEADS2, X_HEADS = 16, 2, 4
FF2 = 2816
XR0, GR0, QQ0, KK0, VV0, GRNN0, GATT0 = 0, 1024, 2048, 3072, 3200, 3328, 4352

SLAB, RING = 1024, 3
TAIL = 2
N_FIRST = 28
N_EXPERT = 6
N_LAYER = 168
FF_HALVES = ((0, 12), (12, 10))
L_BASE = N_FIRST + N_EXPERT * EXPERTS
SLABS = L_BASE + LAYERS * N_LAYER

CONSTS = [("ident", 128), ("rot1", 128), ("dup", 128), ("duprot", 128), ("rot2", 128), ("swap", 128),
          ("tri", 128), ("cmask", 128), ("cmask_t", 128), ("swamask", 256), ("one", 128),
          ("cos1", T), ("sin1", T), ("cos2", T), ("sin2", T)]
NCONST = sum(n for _, n in CONSTS)

LAYER_BARRIERS = 6

PHASE_SEMS = (
    "params_landed",
    "act_link", "dve_link",
    "products",
    "evacuated",
    "banks_read",
    "transposed",
    "hi_ready", "lo_ready",
    "chunk_ready",
    "small_products", "turned",
    "scores", "scores_read", "maxima",
    "probs",
    "sums_inverted", "divided", "divided_too",
    "probs_t", "probs_t_copied",
    "values", "values_read",
    "summed", "variance", "shift_ready",
    "deviation", "normalised",
    "relu", "relu_used",
    "narrow_products", "narrow_copied",
    "taps0", "convolved", "activated",
    "sp_in", "sp_exp", "sp_sum", "sp_log", "sp_done",
    "cumulated", "decay_in", "decays", "tokens_x",
    "cb_products", "decay_masked", "decay_exp", "decayed",
    "chunk_products", "state_ready",
    "gate_in", "gate_exp",
    "gates_full", "ups_full", "downs_full",
    "silu_done", "hidden", "hidden_hi", "hidden_lo",
    "downs_free", "first_half_summed",
    "r_done", "i_done", "i_used", "tanh_done", "decay_done", "mult2", "mult", "gelu_done",
)


def tables():
    c = {}
    eye = np.eye(P, dtype=np.float32)
    c["ident"] = eye
    rot1, rot2, dup, swap = (np.zeros((P, P), np.float32) for _ in range(4))
    for m in range(P):
        d = m % HD
        if d < 32:
            rot1[m + 32, m] = -1.0
        else:
            rot1[m - 32, m] = 1.0
        if d < 8:
            rot2[m + 8, m] = -1.0
        elif d < 16:
            rot2[m - 8, m] = 1.0
        dup[d, m] = 1.0
        swap[(m + HD) % P, m] = 1.0
    c["rot1"], c["rot2"], c["dup"], c["swap"], c["duprot"] = rot1, rot2, dup, swap, dup @ rot1
    i, j = np.arange(P)[:, None], np.arange(P)[None, :]
    c["tri"] = (i <= j).astype(np.float32)
    c["cmask"] = np.where(j <= i, 0.0, NEG).astype(np.float32)
    c["cmask_t"] = np.where(j >= i, 0.0, NEG).astype(np.float32)
    w = np.arange(2 * P)[None, :]
    c["swamask"] = np.where((w > i) & (w <= i + P), 0.0, NEG).astype(np.float32)
    c["one"] = np.ones((P, P), np.float32)
    pos = np.arange(T, dtype=np.float32)
    inv1 = np.float32(10000.0) ** (-np.arange(0, HD, 2, dtype=np.float32) / np.float32(HD))
    ang1 = (pos[:, None] * inv1[None, :]).astype(np.float32)
    c["cos1"] = np.cos(ang1).T[np.arange(P) % 32].astype(np.float32)
    c["sin1"] = np.sin(ang1).T[np.arange(P) % 32].astype(np.float32)
    inv2 = np.float32(500000.0) ** (-np.arange(0, 16, 2, dtype=np.float32) / np.float32(16))
    ang2 = (pos[:, None] * inv2[None, :]).astype(np.float32)
    turned = (np.arange(P) % HD < 16)[:, None]
    c["cos2"] = np.where(turned, np.cos(ang2).T[np.arange(P) % 8], 1.0).astype(np.float32)
    c["sin2"] = np.where(turned, np.sin(ang2).T[np.arange(P) % 8], 0.0).astype(np.float32)
    return np.ascontiguousarray(np.concatenate([c[n] for n, _ in CONSTS], axis=1))


def build(nc, A, out):
    KB = 1024
    top = [(nc.sbuf_base + 63) // 64 * 64]

    def place(name, shape, dtype=F32, offset=None):
        size = 4 * int(np.prod(shape[1:]))
        if offset is None:
            offset, top[0] = top[0], (top[0] + size + 63) // 64 * 64
        else:
            offset = arena + offset * KB
        return nc.alloc_sbuf_tensor_at(name, shape, dtype, offset=offset)

    w_raw = place("w_raw", [P, RING, SLAB])
    w_hi = place("w_hi", [P, RING, SLAB], F32R)
    w_lo = place("w_lo", [P, RING, SLAB], F32R)
    res = place("res", [P, NT, D])
    x_hi = place("x_hi", [P, KD, T], F32R)
    x_lo = place("x_lo", [P, KD, T], F32R)
    const = place("const", [P, NCONST])
    gain = place("gain", [P, 2, D])
    gain_f = place("gain_f", [P, 2, KD])
    taps = place("taps", [P, 4, KD])
    tap_bias = place("tap_bias", [P, KD])
    gate_bias = place("gate_bias", [P, 2, KD])
    lam = place("lam", [P, 8, KD])
    sink = place("sink", [P, Q_HEADS2])
    stats = place("stats", [P, NT, 2, 6])
    mv = place("mv", [P, NT, 2])
    dev = place("dev", [P, NT])
    rdev = place("rdev", [P, NT])
    shift = place("shift", [P, NT])
    nmax = place("nmax", [P, 4, 2])
    den = place("den", [P, 4, 2])
    rden = place("rden", [P, 4, 2])
    vbuf = place("vbuf", [P, 2, T])
    iw = place("iw", [P, NT, I_HEADS])
    top8 = place("top8", [P, 8])
    short = place("short", [P, 1])
    sp = place("sp", [P, 8, 32])
    dt_raw = place("dt_raw", [P, 32])
    dt_a = place("dt_a", [P, 32])
    head_in = place("head_in", [P, 4, 8])
    norm_w = place("norm_w", [P, 4])
    dec = place("dec", [P, 6, 32])
    dec_t = place("dec_t", [P, 32])
    dec4 = place("dec4", [P, NT, 4])
    route_b = place("route_b", [P, 20])
    rt = place("rt", [P, NT, 64])
    gates = place("gates", [P, NT, EXPERTS])
    arena = top[0]
    consts = {}
    at = 0
    for name, width in CONSTS:
        consts[name] = const[:, at:at + width]
        at += width
    ident = consts["ident"]
    ps = nc.alloc_psum_tensor("ps", [P, 8, 512], F32)

    pf = place("pf", [P, 14, T], F32, 0)
    zt = place("zt", [P, NT, 512], F32, 30)
    mb = place("mb", [P, NT, T], F32, 38)
    sc1 = place("sc1", [P, 2, 2, T], F32, 46)
    pt1 = place("pt1", [P, 2, 2, T], F32, 54)
    ot1 = place("ot1", [P, NT, D], F32, 62)
    vt1 = place("vt1", [P, NT, HD], F32, 78)
    ix = place("ix", [P, 4, T], F32, 46)
    rl = place("rl", [P, 4, T], F32, 54)
    ones = place("ones", [P, T], F32, 62)
    kz = place("kz", [P, 2, T], F32, 79)
    iz = place("iz", [P, 2, T], F32, 83)
    cz = place("cz", [P, 2, T], F32, 56)
    narrow_f = place("narrow_f", [20, T], F32, 64)
    xc1 = place("xc1", [P, 6, T], F32, 79)
    xt1 = place("xt1", [P, NT, 512], F32, 46)
    bt1 = place("bt1", [P, NT, P], F32, 54)
    xdt = place("xdt", [P, NT, 512], F32, 0)
    lm = place("lm", [P, 2, 4, P], F32, 8)
    prev = place("prev", [P, 256], F32, 12)
    yt = place("yt", [P, 512], F32, 13)
    xsk = place("xsk", [P, NT, 512], F32, 16)
    sq = place("sq", [P, 512], F32, 24)
    xdec = place("xdec", [P, NT, 512], F32, 38)
    oh1 = place("oh1", [P, KD, T], F32R, 0)
    ol1 = place("ol1", [P, KD, T], F32R, 16)
    eh = place("eh", [P, 2, T], F32R, 0)
    el = place("el", [P, 2, T], F32R, 4)
    esg = place("esg", [P, 2, T], F32, 8)
    ehd = place("ehd", [P, 2, T], F32, 12)
    qf = place("qf", [P, 8, T], F32, 0)
    kr = place("kr", [P, T], F32, 16)
    ks = place("ks", [P, 4, T], F32, 40)
    vr = place("vr", [P, T], F32, 22)
    vt2 = place("vt2", [P, NT, P], F32, 24)
    sc2 = place("sc2", [P, 4, 2, 257], F32, 26)
    pt2 = place("pt2", [P, 2, 2, 256], F32, 35)
    oh2 = place("oh2", [P, KD, T], F32R, 50)
    ol2 = place("ol2", [P, KD, T], F32R, 66)
    sgm = place("sgm", [P, 2, T], F32, 82)
    mg = place("mg", [P, KD, T], F32, 0)
    gg = place("gg", [P, KD, T], F32, 50)
    xc2 = place("xc2", [P, KD, T], F32, 16)
    yh = place("yh", [P, KD, T], F32R, 34)
    yl = place("yl", [P, KD, T], F32R, 50)
    ga = place("ga", [P, KD, T], F32, 66)
    t8 = place("t8", [P, KD, T], F32, 34)
    t4 = place("t4", [P, 4, T], F32, 82)
    mh = place("mh", [P, KD, T], F32R, 66)
    ml = place("ml", [P, KD, T], F32R, 16)
    mt = place("mt", [P, 2, D], F32, 0)
    mem_h = place("mem_h", [P, KD, MEM], F32R, 8)
    mem_l = place("mem_l", [P, KD, MEM], F32R, 16)
    kc = place("kc", [P, KD, MEM], F32, 24)
    vc = place("vc", [P, 2, D], F32, 32)
    qc = place("qc", [P, KD, T], F32, 40)
    sc3 = place("sc3", [P, 2, 2, 256], F32, 56)
    pt3 = place("pt3", [P, 2, 2, 256], F32, 60)
    ot3 = place("ot3", [P, NT, D], F32, 64)
    oh3 = place("oh3", [P, KD, T], F32R, 0)
    ol3 = place("ol3", [P, KD, T], F32R, 16)
    fh = place("fh", [P, 12, T], F32R, 0)
    fl = place("fl", [P, 12, T], F32R, 24)
    fsg = place("fsg", [P, 2, 2, T], F32, 48)
    fhd = place("fhd", [P, 2, T], F32, 56)

    UNITS1 = [(i, p) for i in range(NT) for p in range(A_HEADS // 2)]
    UNITS2 = [(i, p) for i in range(NT) for p in range(Q_HEADS2 // 2)]
    UNITS3 = [(i, p) for i in range(NT) for p in range(X_HEADS // 2)]

    def width1(unit):
        return (unit[0] + 1) * P

    def width2(unit):
        return 2 * P if unit[0] else P

    def width3(unit):
        return MEM

    def transposed_bank(u, h, by_head):
        return ps[:, 4 + h, :] if by_head else ps[:, 4 + u % 2, 256 * h:256 * h + 256]

    def values_bank(u):
        return ps[:, 6 + u % 2, :]

    with ExitStack() as ctx:
        def sem(name):
            return ctx.enter_context(nc.semaphore(name))

        s = {name: sem(name) for name in PHASE_SEMS}
        nums = sorted(v.num for v in s.values())
        assert nums == list(range(nums[0], nums[0] + len(nums)))
        phase_range = range(nums[0], nums[-1] + 1)
        raw_landed = [sem(f"raw_landed{i}") for i in range(RING)]
        hi_done, lo_done, slab_used = sem("hi_done"), sem("lo_done"), sem("slab_used")
        arrived, stored, start, loads_begun = sem("arrived"), sem("stored"), sem("start"), sem("loads_begun")
        first_landed, x_landed = sem("first_landed"), [sem("x_landed0"), sem("x_landed1")]
        go = [sem("go_even"), sem("go_odd")]
        finished = sem("finished")
        block = ctx.enter_context(nc.Block())

        class Count:
            def __init__(self):
                self.n, self.base, self.turns, self.looped = 0, 0, 0, False

            def at(self, more):
                return self.base + (self.n + more) if self.looped else self.n + more

            def enter(self, base, turns=0):
                self.base, self.turns, self.looped = base, turns, True

            def leave(self):
                self.base, self.turns, self.looped = 0, 0, False

        def view(w):
            return w.rearrange("(k p) n -> p k n", p=P)

        def f_pair(v, c0, width=256):
            for h in range(2):
                yield v[:, 4 * h:4 * h + 4, c0:c0 + width]

        def rows(v, ks_, c0=0):
            for k in ks_:
                yield v[:, k:k + 1, c0:c0 + D]

        def slabs_first():
            w = view(A["w_in"][0])
            for c0, n in ((Q0, 256), (Q0 + 256, 256), (KV0, 256), (IQ0 + 128, 196)):
                yield from f_pair(w, c0, n)
            for c0 in (XBC0, XBC0 + 256, XBC0 + 512):
                yield from f_pair(w, c0)
            yield w[:, :, DT0:DT0 + 8]
            for h in range(4):
                yield w[:, 2 * h:2 * h + 2, Z0:Z0 + 512]
            yield from rows(view(A["w_out"][0]), range(KD))
            yield view(A["w_route"][0])

        def expert_up(e):
            for w in (A["w_gate"], A["w_up"]):
                yield from f_pair(view(w[0][e]), 0)

        def expert_down(e):
            v = view(A["w_down"][0][e])
            for h in range(2):
                yield v[:, :, 512 * h:512 * h + 512]

        def layer_slabs(l):
            w = view(A["w_in_2"][l])
            for c0 in [KK0, *range(QQ0, KK0, 256)]:
                yield from f_pair(w, c0)
            for p in range(4):
                yield from f_pair(w, GATT0 + 256 * p)
                yield from f_pair(view(A["w_br_attn_2"][l]), 256 * p)
            for p in range(4):
                yield from f_pair(w, XR0 + 256 * p)
            for name in ("w_rg_2", "w_ig_2"):
                v = A[name][l].rearrange("b (k p) n -> p (b k) n", p=P)
                for h in range(2):
                    yield v[:, 4 * h:4 * h + 4, :]
            for p in range(4):
                yield from f_pair(w, GR0 + 256 * p)
            gate, branch = GRNN0, view(A["w_br_rnn_2"][l])
            for p in range(2):
                yield from f_pair(w, gate + 256 * p)
            for p in range(2):
                yield from f_pair(branch, 256 * p)
            for p in range(2, 4):
                yield from f_pair(w, gate + 256 * p)
                yield from f_pair(branch, 256 * p)
            yield from rows(view(A["w_out_2"][l]), range(KD))
            for p in range(4):
                yield from f_pair(view(A["cq_w_2"][l]), 256 * p)
            for p in range(4):
                yield from f_pair(view(A["ckv_w_2"][l]), 256 * p)
            yield from rows(view(A["ckv_w_2"][l]), range(KD), D)
            yield from rows(view(A["co_w_2"][l]), range(KD))
            wi, wo = view(A["ffn_wi_2"][l]), view(A["ffn_wo_2"][l])
            for c0, n in FF_HALVES:
                for p in range(n // 2):
                    yield from f_pair(wi, 128 * c0 + 256 * p)
                    yield from f_pair(wi, FF2 + 128 * c0 + 256 * p)
                yield from rows(wo, range(c0, c0 + n))

        @block.sync
        def _(sync):
            slab = Count()

            def load(src):
                slot = slab.n % RING
                if slab.looped or slab.n >= RING:
                    sync.wait_ge(lo_done, slab.at(1 - RING))
                    if slab.looped:
                        sync.sem_inc(loads_begun, 1)
                k, n = src.shape[1], src.shape[2]
                sync.dma_start(w_raw[:, slot, :k * n].rearrange("p (k n) -> p k n", k=k), src)\
                    .then_inc(raw_landed[slot], 16)
                slab.n += 1

            for src in [*slabs_first(), *expert_up(0)]:
                load(src)
            assert slab.n == N_FIRST + 4
            with sync.Fori(0, EXPERTS - 1) as e:
                slab.enter(e * N_EXPERT)
                for src in [*expert_up(e + 1), *expert_down(e)]:
                    load(src)
            slab.leave()
            slab.n += (EXPERTS - 2) * N_EXPERT
            for src in expert_down(EXPERTS - 1):
                load(src)
            assert slab.n == L_BASE
            with sync.Fori(0, LAYERS) as l:
                slab.enter(l * N_LAYER)
                for src in layer_slabs(l):
                    load(src)
            assert slab.n == L_BASE + N_LAYER, slab.n
            sync.wait_ge(finished, 1)
            sync.dma_start(out[0].rearrange("(t p) d -> p t d", p=P), res[:, :, :]).then_inc(stored, 16)
            sync.wait_ge(stored, 16)

        @block.gpsimd
        def _(pool):
            def low(slot, value):
                pool.wait_ge(hi_done, value)
                pool.tensor_tensor(w_lo[:, slot, :], w_raw[:, slot, :], w_hi[:, slot, :].bitcast(F32),
                                   ALU.subtract).then_inc(lo_done, 1)

            with pool.Fori(0, SLABS // RING) as g:
                for i in range(RING):
                    low(i, g * RING + (i + 1))
            for n in range(SLABS // RING * RING, SLABS):
                low(n % RING, n + 1)

        @block.tensor
        def _(pe):
            slab, phase = Count(), Count()
            used_later = [False]

            def mm(o, a, b, first=True, last=True, inc=None):
                ins = pe.matmul(o, a, b, start=first, stop=last)
                if inc is not None:
                    assert not used_later[0]
                    ins.then_inc(s[inc], 1)
                elif used_later[0]:
                    ins.then_inc(slab_used, 1)
                    used_later[0] = False
                return ins

            def flip(o, a, inc=None):
                n = a.shape[0]
                ins = pe.transpose(o, a, ident[:n, :n])
                if inc is not None:
                    assert not used_later[0]
                    ins.then_inc(s[inc], 1)
                elif used_later[0]:
                    ins.then_inc(slab_used, 1)
                    used_later[0] = False

            def flush():
                if used_later[0]:
                    pe.drain().then_inc(slab_used, 1)
                    used_later[0] = False

            def barrier():
                flush()
                pe.drain().then_inc(arrived, 1)
                pe.wait_ge(go[phase.n % 2], 1)
                pe.drain()
                phase.n += 1

            def take():
                pe.wait_ge(lo_done, slab.at(1))
                slab.n += 1
                return (slab.n - 1) % RING

            def three(o, ah, al, bh, bl, first, last, inc=None):
                mm(o, ah, bh, first, False)
                mm(o, al, bh, False, False)
                return mm(o, ah, bl, False, last, inc)

            def three_t(o, xh, xl, wh, wl, first, last, inc=None):
                mm(o, xh, wh, first, False)
                mm(o, xh, wl, False, False)
                return mm(o, xl, wh, False, last, inc)

            def pair_f(banks, xh, xl, width=256, nt=T, inc="products", follow=False, base=0):
                if follow:
                    order = ((0, 0), (0, 1), (1, 0), (1, 1), (0, 2), (1, 2), (0, 3), (1, 3))
                else:
                    order = tuple((c, kk) for c in range(2) for kk in range(4))
                for h in range(2):
                    slot = take()
                    for c, kk in order:
                        m = (P, width - P)[c]
                        k, col, end = 4 * h + kk, kk * width + c * P, kk == 3
                        if follow and c == 0:
                            pe.wait_ge(s["lo_ready"], base + k + 1)
                        ins = three(ps[:m, banks[c], 0:nt], w_hi[:, slot, col:col + m], w_lo[:, slot, col:col + m],
                                    xh[:, k, 0:nt], xl[:, k, 0:nt], k == 0, k == 7,
                                    inc if (h == 1 and end) else None)
                        if h == 0 and (c, kk) == order[-1]:
                            ins.then_inc(slab_used, 1)
                used_later[0] = True

            def rows_t(xh, xl, n, tiles=NT, norm=True):
                def part(t, half, k, slot):
                    tk, wk = slice(t * P, t * P + P), slice(512 * half, 512 * half + 512)
                    return three_t(ps[:, 2 * t + half, :], xh[:, k, tk], xl[:, k, tk], w_hi[:, slot, wk],
                                   w_lo[:, slot, wk], k == 0, k == n - 1,
                                   "products" if (k == n - 1 and half == 1) else None)

                single = n - TAIL if norm else n
                for k in range(single):
                    slot = take()
                    for t in range(tiles):
                        for half in range(2):
                            ins = part(t, half, k, slot)
                    if k < n - 1:
                        ins.then_inc(slab_used, 1)
                used_later[0] = not norm
                if norm:
                    slots = [take() for _ in range(TAIL)]
                    for t in range(tiles):
                        for half in range(2):
                            for i, slot in enumerate(slots):
                                part(t, half, single + i, slot)
                    pe.drain().then_inc(slab_used, TAIL)

            def narrow(bank, width, follow=False):
                slot = take()
                for k in range(KD):
                    col = k * width
                    if follow:
                        pe.wait_ge(s["lo_ready"], k + 1)
                    three(ps[:, bank, :], w_hi[:, slot, col:col + P], w_lo[:, slot, col:col + P], x_hi[:, k, :],
                          x_lo[:, k, :], k == 0, k == KD - 1, "narrow_products" if k == KD - 1 else None)
                used_later[0] = True

            def narrow_to_tokens(bank, width):
                pe.wait_ge(s["narrow_copied"], 1)
                for t in range(NT):
                    flip(ps[:, bank, t * 32:t * 32 + width], narrow_f[0:width, t * P:t * P + P],
                         "narrow_products" if t == NT - 1 else None)

            def to_features(src, tiles=NT, second=None):
                for k in range(KD):
                    if second is not None and k == KD // 2:
                        pe.wait_ge(second, 16)
                    for t in range(tiles):
                        flip(ps[:, k, t * P:t * P + P], src[:, t, k * P:k * P + P],
                             "transposed" if t == tiles - 1 else None)

            def normed_to_features(banks_in_use=True):
                if banks_in_use:
                    pe.wait_ge(s["summed"], NT)
                for t in range(NT):
                    pe.wait_ge(s["normalised"], t + 1)
                    for k in range(KD):
                        flip(ps[:, k, t * P:t * P + P], res[:, t, k * P:k * P + P],
                             "transposed" if t == NT - 1 else None)

            def attention(units, width, sc, pt, scores_of, values_of, by_head=False):
                last = len(units) - 1

                def scores(u):
                    if u > last:
                        return
                    if u >= 2:
                        pe.wait_ge(s["scores_read"], u - 1)
                    scores_of(u, units[u])

                def transposes(u):
                    n = width(units[u]) // P
                    pe.wait_ge(s["probs"], 2 * u + 2)
                    for h in range(2):
                        item = 2 * u + h if by_head else u
                        if item >= 2 and (by_head or h == 0):
                            pe.wait_ge(s["probs_t_copied"], item - 1)
                        for j in range(n):
                            flip(transposed_bank(u, h, by_head)[:, j * P:j * P + P], sc[:, u % 2, h, j * P:j * P + P],
                                 "probs_t" if (j == n - 1 and (by_head or h == 1)) else None)

                def values(u):
                    n = width(units[u]) // P
                    pe.wait_ge(s["probs_t_copied"], 2 * (u + 1) if by_head else u + 1)
                    if u >= 2:
                        pe.wait_ge(s["values_read"], u - 1)
                    for h in range(2):
                        for j in range(n):
                            v = values_of(units[u], h, j)
                            dv = v.shape[-1]
                            mm(values_bank(u)[:, h * dv:h * dv + dv], pt[:, u % 2, h, j * P:j * P + P], v,
                               j == 0, j == n - 1, "values" if (h == 1 and j == n - 1) else None)

                scores(0)
                scores(1)
                for u in range(last + 1):
                    transposes(u)
                    scores(u + 2)
                    if u >= 1:
                        values(u - 1)
                values(last)

            pe.wait_ge(x_landed[0], 16)
            pe.wait_ge(first_landed, 16)
            to_features(res, second=x_landed[1])
            barrier()
            for p in range(4):
                pair_f((2 * p, 2 * p + 1), x_hi, x_lo, 196 if p == 3 else 256)
            barrier()
            for j, c in enumerate((0, 1, 2, 3, 5, 6)):
                mm(ps[:, j, :], consts["rot1"], pf[:, c, :], inc="products")
            mm(ps[:, 6, :], consts["dup"], pf[:, 4, :], inc="products")
            mm(ps[:, 7, :], consts["duprot"], pf[:, 4, :], inc="products")
            pe.wait_ge(s["banks_read"], 1)
            mm(ps[:, 0, :], consts["dup"][:68, :], pf[:68, 7, :], inc="products")
            pe.wait_ge(s["banks_read"], 2)
            mm(ps[:, 1, :], consts["duprot"][:68, :], pf[:68, 7, :], inc="products")
            pe.wait_ge(s["banks_read"], 3)
            for t in range(NT):
                flip(ps[:, 2, t * P:t * P + P], pf[:, 4, t * P:t * P + P], "products" if t == NT - 1 else None)
            pe.wait_ge(s["banks_read"], 4)
            for t in range(NT):
                flip(ps[:, 3, t * P:t * P + 68], pf[:68, 7, t * P:t * P + P], "products" if t == NT - 1 else None)
            barrier()
            for i in range(1, NT):
                for h in range(I_HEADS):
                    if i >= 2:
                        pe.wait_ge(s["relu"], 4 * (i - 2) + h + 1)
                    mm(ps[:, h, 0:(i + 1) * P], pf[:, 5 + h // 2, i * P:i * P + P],
                       iz[:, h % 2, 0:(i + 1) * P], inc="scores")
            pe.wait_ge(s["relu"], 4 * (NT - 1))
            for p in range(3):
                pair_f((2 * p, 2 * p + 1), x_hi, x_lo)
            narrow(6, 8)
            pe.wait_ge(s["evacuated"], 4)
            for j in range(4):
                slot = take()
                for t in range(NT):
                    for kk in range(2):
                        k, tk, wk = 2 * j + kk, slice(t * P, t * P + P), slice(kk * 512, kk * 512 + 512)
                        ins = three_t(ps[:, t, :], x_hi[:, k, tk], x_lo[:, k, tk], w_hi[:, slot, wk],
                                      w_lo[:, slot, wk], k == 0, k == 7, "products" if k == 7 else None)
                if j < 3:
                    ins.then_inc(slab_used, 1)
            pe.drain().then_inc(slab_used, 1)
            narrow_to_tokens(7, 8)
            barrier()

            def scores1(u, unit):
                i, p = unit
                for h in range(2):
                    mm(ps[:, 2 * (u % 2) + h, 0:width1(unit)], pf[:, p, i * P:i * P + P],
                       kz[:, h, 0:width1(unit)], inc="scores" if h == 1 else None)

            attention(UNITS1, width1, sc1, pt1, scores1, lambda unit, h, j: vt1[:, j, :], by_head=True)
            barrier()
            for c in range(5):
                pe.wait_ge(s["activated"], c + 1)
                for t in range(NT):
                    flip(ps[:, c, t * P:t * P + P], xc1[:, c, t * P:t * P + P], "transposed" if t == NT - 1 else None)
            pe.wait_ge(s["sp_done"], 1)
            mm(ps[:, 5, 0:32], consts["tri"], dt_a[:, :])
            mm(ps[:, 6, 0:32], consts["one"], dt_a[:, :], inc="cumulated")
            barrier()
            for c in range(NT):
                tk = slice(c * P, c * P + P)
                for g in range(S_GROUPS):
                    j = 2 * c + g
                    if c >= 1:
                        pe.wait_ge(s["decayed"], j - 1)
                    mm(ps[:, g, 0:P], xc1[:, 4, tk], cz[:, g, tk])
                    for h in range(4):
                        col = c * 8 + g * 4 + h
                        mm(ps[:, 2 + g, h * P:h * P + P], dt_a[:, col:col + 1].broadcast_to([P, P]), consts["tri"],
                           inc="cb_products" if h == 3 else None)
                if c >= 1:
                    pe.wait_ge(s["state_ready"], c)
                for g in range(S_GROUPS):
                    r = slice(HD * g, HD * g + HD)
                    mm(ps[:, 5 + 2 * g, 0:256], cz[:, g, tk], prev[:, :])
                    mm(ps[r, 6, 0:256], bt1[:, c, g * HD:g * HD + HD], xdec[:, c, g * 256:g * 256 + 256])
                for g in range(S_GROUPS):
                    pe.wait_ge(s["decayed"], 2 * c + g + 1)
                    for h in range(4):
                        q = (g * 4 + h) * HD
                        mm(ps[:, 4, q:q + HD], lm[:, g, h, :], xdt[:, c, q:q + HD],
                           inc="chunk_products" if (h == 3 and g == 1) else None)
            barrier()
            to_features(ot1)
            barrier()
            rows_t(oh1, ol1, KD)
            normed_to_features()
            narrow(0, 20, follow=True)
            flush()
            narrow_to_tokens(7, 20)

            def up(e):
                if e is not None:
                    pe.wait_ge(s["silu_done"], 2 * e + 2)
                pair_f((0, 1), x_hi, x_lo, inc="gates_full")
                if e is not None:
                    pe.wait_ge(s["hidden"], 2 * e + 2)
                pair_f((2, 3), x_hi, x_lo, inc="ups_full")

            def down(e):
                flush()
                pe.wait_ge(s["hidden_lo"], 2 * e + 2)
                for half in range(2):
                    slot = take()
                    for t in range(NT):
                        pe.wait_ge(s["downs_free"], 8 * e + (4 * half + t + 1))
                        tk = slice(t * P, t * P + P)
                        for k in range(2):
                            wk = slice(k * 512, k * 512 + 512)
                            three_t(ps[:, 4 + t, :], eh[:, k, tk], el[:, k, tk], w_hi[:, slot, wk], w_lo[:, slot, wk],
                                    k == 0, k == 1, "downs_full" if k == 1 else None)
                    used_later[0] = True

            up(None)
            pe.wait_ge(s["evacuated"], 1)
            pe.sem_inc(s["downs_free"], 4)
            with pe.Fori(0, EXPERTS - 1) as e:
                slab.enter(e * N_EXPERT)
                up(e)
                down(e)
            slab.leave()
            slab.n += (EXPERTS - 2) * N_EXPERT
            down(EXPERTS - 1)
            barrier()
            pe.sem_inc(s["products"], NT)

            with pe.Fori(0, LAYERS) as l:
                slab.enter(l * N_LAYER)
                n0, b0 = slab.n, phase.n
                normed_to_features(banks_in_use=False)
                smalls = [0]

                def small_bank():
                    n = smalls[0]
                    smalls[0] += 1
                    if n >= 2:
                        pe.wait_ge(s["banks_read"], n - 1)
                    return ps[:, 6 + n % 2, :]

                def turn(source, evacuated):
                    bank = small_bank()
                    pe.wait_ge(s["evacuated"], evacuated)
                    mm(bank, consts["rot2"], source, inc="small_products")

                pair_f((0, 1), x_hi, x_lo, follow=True)
                pair_f((2, 3), x_hi, x_lo)
                flush()
                turn(kr[:, :], 1)
                pe.wait_ge(s["evacuated"], 2)
                bank = small_bank()
                for t in range(NT):
                    flip(bank[:, t * P:t * P + P], vr[:, t * P:t * P + P], "small_products" if t == NT - 1 else None)
                pair_f((4, 5), x_hi, x_lo)
                flush()
                bank = small_bank()
                pe.wait_ge(s["turned"], 1)
                mm(bank, consts["swap"], kr[:, :], inc="small_products")
                for p in range(4):
                    if p < 2:
                        pe.wait_ge(s["evacuated"], 2 * p + 2)
                        pair_f((2 * p, 2 * p + 1), x_hi, x_lo)
                        flush()
                    for c in (2 * p, 2 * p + 1):
                        turn(qf[:, c, :], 3 + c)
                pe.wait_ge(s["turned"], 9)

                def scores2(u, unit):
                    i, p = unit
                    lo, w = max(i - 1, 0) * P, width2(unit)
                    for h in range(2):
                        mm(ps[:, 2 * (u % 2) + h, 0:w], qf[:, p, i * P:i * P + P],
                           ks[:, 2 * (p // 4) + h, lo:lo + w], inc="scores" if h == 1 else None)

                last = len(UNITS2) - 1

                def window_scores(u):
                    if u <= last:
                        if u >= 2:
                            pe.wait_ge(s["scores_read"], u - 1)
                        scores2(u, UNITS2[u])

                def window_values(u):
                    (i, p), n = UNITS2[u], width2(UNITS2[u]) // P
                    kv = HD * (p // 4)
                    pe.wait_ge(s["probs_t_copied"], u + 1)
                    if u >= 2:
                        pe.wait_ge(s["values_read"], u - 1)
                    for h in range(2):
                        for j in range(n):
                            mm(ps[HD * h:HD * h + HD, 6 + u % 2, 0:P], vt2[:, max(i - 1, 0) + j, kv:kv + HD],
                               pt2[:, u % 2, h, j * P:j * P + P], j == 0, j == n - 1,
                               "values" if (h == 1 and j == n - 1) else None)

                for u in range(3):
                    window_scores(u)
                for u in range(last + 1):
                    n = width2(UNITS2[u]) // P
                    if u >= 2:
                        pe.wait_ge(s["probs_t_copied"], u - 1)
                    for h in range(2):
                        pe.wait_ge(s["divided" if h == 0 else "divided_too"], u + 1)
                        for j in range(n):
                            flip(transposed_bank(u, h, False)[:, j * P:j * P + P], sc2[:, u % 4, h, j * P:j * P + P],
                                 "probs_t" if (j == n - 1 and h == 1) else None)
                    window_scores(u + 3)
                    if u >= 1:
                        window_values(u - 1)
                window_values(last)
                barrier()

                for p in range(4):
                    b = 4 * (p % 2)
                    if p >= 2:
                        pe.wait_ge(s["evacuated"], 2 * (p - 1))
                    pair_f((b, b + 1), x_hi, x_lo)
                    if p >= 2:
                        pe.wait_ge(s["banks_read"], 2 * (p - 1))
                    pair_f((b + 2, b + 3), oh2, ol2)
                barrier()
                for p in range(4):
                    pair_f((2 * p, 2 * p + 1), x_hi, x_lo)
                flush()
                for g in range(2):
                    for h in range(2):
                        slot = take()
                        for q in range(4):
                            blk, c = q // 2, q % 2
                            j = 4 * h + q
                            pe.wait_ge(s["r_done" if g else "taps0"], j + 1)
                            for kk in range(2):
                                k, col = 4 * h + 2 * blk + kk, (2 * blk + kk) * 256 + c * P
                                if g == 0 and c == 0:
                                    pe.wait_ge(s["lo_ready"], k + 1)
                                three(ps[:, j, :], w_hi[:, slot, col:col + P], w_lo[:, slot, col:col + P],
                                      yh[:, k, :], yl[:, k, :], kk == 0, kk == 1, "products" if kk == 1 else None)
                        used_later[0] = True
                for p in range(4):
                    pe.wait_ge(s["i_done"], 2 * p + 2)
                    pair_f((2 * p, 2 * p + 1), x_hi, x_lo)
                for p in range(2):
                    pe.wait_ge(s["gelu_done"], 4 * p + 2)
                    pair_f((4 * p, 4 * p + 1), x_hi, x_lo)
                barrier()
                for p in range(4):
                    b = 4 * (p % 2)
                    if p >= 2:
                        pe.wait_ge(s["evacuated"], 2 * (p - 1))
                        pair_f((b, b + 1), x_hi, x_lo)
                        pe.wait_ge(s["banks_read"], 2 * (p - 1))
                    pair_f((b + 2, b + 3), yh, yl)
                barrier()
                rows_t(mh, ml, KD)
                normed_to_features()
                for p in range(4):
                    pair_f((2 * p, 2 * p + 1), x_hi, x_lo, follow=p == 0)
                pe.wait_ge(s["evacuated"], 8)
                to_features(mt, tiles=2)
                for p in range(4):
                    pair_f((2 * p, 2 * p + 1), mem_h, mem_l, nt=MEM, follow=p == 0, base=KD)
                pe.wait_ge(s["evacuated"], 8 + 4)
                rows_t(mem_h, mem_l, KD, tiles=2, norm=False)
                barrier()

                def scores3(u, unit):
                    i, p = unit
                    for h in range(2):
                        for k in range(2):
                            c = 2 * (2 * p + h) + k
                            mm(ps[:, 2 * (u % 2) + h, 0:MEM], qc[:, c, i * P:i * P + P], kc[:, c, :],
                               k == 0, k == 1, "scores" if (h == 1 and k == 1) else None)

                def values3(unit, h, j):
                    head = 2 * unit[1] + h
                    return vc[:, j, 256 * head:256 * head + 256]

                attention(UNITS3, width3, sc3, pt3, scores3, values3)
                pe.wait_ge(s["values_read"], len(UNITS3))
                to_features(ot3)
                pe.wait_ge(s["lo_ready"], KD)
                rows_t(oh3, ol3, KD)
                normed_to_features()
                pairs = 0
                for half, (c0, n) in enumerate(FF_HALVES):
                    for p in range(n // 2):
                        b = 4 * (pairs % 2)
                        if half and p < 2:
                            pe.wait_ge(s["first_half_summed"], 2 * p + 1)
                        elif p >= 2:
                            pe.wait_ge(s["silu_done"], 2 * (pairs - 1))
                        pair_f((b, b + 1), x_hi, x_lo, inc="gates_full", follow=pairs == 0, base=KD)
                        if half and p < 2:
                            pe.wait_ge(s["first_half_summed"], 2 * p + 2)
                        elif p >= 2:
                            pe.wait_ge(s["hidden"], 2 * (pairs - 1))
                        pair_f((b + 2, b + 3), x_hi, x_lo, inc="ups_full")
                        pairs += 1
                    flush()
                    pe.wait_ge(s["hidden_lo"], 2 * pairs)
                    if half:
                        barrier()
                    rows_t(fh, fl, n, norm=half == 1)
                pe.wait_ge(s["summed"], NT)
                assert (slab.n - n0, phase.n - b0) == (N_LAYER, LAYER_BARRIERS), (slab.n - n0, phase.n - b0)

        @block.scalar
        def _(act):
            slab, phase = Count(), Count()
            links = [0]

            def link(ins):
                links[0] += 1
                ins.then_inc(s["act_link"], 1)
                act.wait_ge(s["act_link"], links[0])

            def barrier():
                act.drain().then_inc(arrived, 1)
                act.wait_ge(go[phase.n % 2], 1)
                act.drain()
                phase.n += 1
                links[0] = 0

            def split(count):
                for _ in range(count):
                    n = slab.n
                    act.wait_ge(raw_landed[n % RING], slab.turns * 16 + 16 * (n // RING + 1))
                    if slab.looped or n >= RING:
                        act.wait_ge(slab_used, slab.at(1 - RING))
                    act.activation(w_hi[:, n % RING, :], w_raw[:, n % RING, :], ACT.Copy).then_inc(hi_done, 1)
                    slab.n += 1

            def load(*pairs):
                for dst, src in pairs:
                    act.dma_start(dst, src).then_inc(s["params_landed"], 16)

            def high_parts(hi, nt=T, affine=None, base=0):
                for k in range(KD):
                    act.wait_ge(s["transposed"], base + k + 1)
                    if affine is None:
                        act.activation(hi[:, k, 0:nt], ps[:, k, 0:nt], ACT.Copy).then_inc(s["hi_ready"], 1)
                        continue
                    g, b = affine(k)
                    if k >= 2:
                        act.wait_ge(s["lo_ready"], base + k - 1)
                    link(act.activation(vbuf[:, k % 2, 0:nt], ps[:, k, 0:nt], ACT.Identity, scale=g, bias=b))
                    act.activation(hi[:, k, 0:nt], vbuf[:, k % 2, 0:nt], ACT.Copy).then_inc(s["hi_ready"], 1)

            def attention(units, width, sc, pt, by_head=False):
                def exps(u):
                    w = width(units[u])
                    act.wait_ge(s["maxima"], u + 1)
                    if u >= 4:
                        act.wait_ge(s["values_read"], u - 3)
                    for h in range(2):
                        act.activation(sc[:, u % 2, h, 0:w], sc[:, u % 2, h, 0:w], ACT.Exp,
                                       bias=nmax[:, u % 4, h:h + 1], accum_out=den[:, u % 4, h:h + 1])\
                           .then_inc(s["probs"], 1)

                exps(0)
                for u, unit in enumerate(units):
                    if u + 1 < len(units):
                        exps(u + 1)
                    w = width(unit)
                    if u >= 2:
                        act.wait_ge(s["values"], u - 1)
                    if by_head:
                        for h in range(2):
                            act.wait_ge(s["probs_t"], 2 * u + h + 1)
                            act.activation(pt[:, u % 2, h, 0:w], transposed_bank(u, h, True)[:, 0:w], ACT.Copy)\
                               .then_inc(s["probs_t_copied"], 1)
                    else:
                        act.wait_ge(s["probs_t"], u + 1)
                        src = ps[:, 4 + u % 2, :].rearrange("p (h n) -> p h n", h=2)
                        act.activation(pt[:, u % 2, :, 0:w], src[:, :, 0:w], ACT.Copy)\
                           .then_inc(s["probs_t_copied"], 1)

            def softplus(e, x, log, u):
                act.wait_ge(s["sp_in"], 1)
                act.activation(e, x, ACT.Exp, scale=-1.0).then_inc(s["sp_exp"], 1)
                act.wait_ge(s["sp_sum"], 1)
                act.activation(log, u, ACT.Ln).then_inc(s["sp_log"], 1)

            def per_feature(name, l):
                return A[name + "_f"][l]

            def load_norm(g, b, l):
                load((gain[:, 0, :], A[g][l].partition_broadcast(P)), (gain[:, 1, :], A[b][l].partition_broadcast(P)),
                     (gain_f[:, 0, :], per_feature(g, l)), (gain_f[:, 1, :], per_feature(b, l)))

            def normalise_tiles():
                def normalise(t):
                    act.wait_ge(s["shift_ready"], t + 1)
                    act.activation(res[:, t, :], res[:, t, :], ACT.Identity, scale=rdev[:, t:t + 1],
                                   bias=shift[:, t:t + 1]).then_inc(s["normalised"], 1)

                for t in range(NT):
                    act.wait_ge(s["variance"], t + 1)
                    act.activation(dev[:, t:t + 1], mv[:, t, 1:2], ACT.Sqrt).then_inc(s["deviation"], 1)
                    if t:
                        normalise(t - 1)

            def norm_high_parts(base=0):
                high_parts(x_hi, affine=lambda k: (gain_f[:, 0, k:k + 1], gain_f[:, 1, k:k + 1]), base=base)

            act.dma_start(const[:, 0:P], A["tables"][:, 0:P]).then_inc(first_landed, 16)
            x = A["x"][0].rearrange("(t p) d -> p t d", p=P)
            for h in range(2):
                act.dma_start(res[:, :, 512 * h:512 * h + 512], x[:, :, 512 * h:512 * h + 512]).then_inc(x_landed[h], 16)
            act.dma_start(const[:, P:NCONST], A["tables"][:, P:NCONST]).then_inc(start, 16)
            high_parts(x_hi)
            split(RING)
            act.wait_ge(start, 16)
            barrier()
            for j in range(8):
                m = 68 if j == 7 else P
                act.wait_ge(s["products"], j + 1)
                act.activation(pf[:m, j, :], ps[:m, j, :], ACT.Copy).then_inc(s["evacuated"], 1)
                if j % 2:
                    split(2)
            barrier()
            act.wait_ge(s["products"], 11)
            tv = ps[:, 2, :].rearrange("p (t n) -> p t n", t=NT)
            act.activation(vt1[:, :, :], tv[:, :, HD:2 * HD], ACT.Copy)
            act.wait_ge(s["products"], 12)
            tw = ps[:, 3, :].rearrange("p (t n) -> p t n", t=NT)
            act.activation(iw[:, :, :], tw[:, :, 64:68], ACT.Copy, scale=IDX_SCALE)
            barrier()
            for i in range(1, NT):
                w = (i + 1) * P
                for h in range(I_HEADS):
                    act.wait_ge(s["scores"], 4 * (i - 1) + h + 1)
                    if i >= 2:
                        act.wait_ge(s["relu_used"], 4 * (i - 2) + h + 1)
                    act.activation(rl[:, h, 0:w], ps[:, h, 0:w], ACT.Relu).then_inc(s["relu"], 1)
            for j in range(6):
                act.wait_ge(s["products"], j + 1)
                act.activation(pf[:, 8 + j, :], ps[:, j, :], ACT.Copy).then_inc(s["evacuated"], 1)
                if j % 2:
                    split(2)
            act.wait_ge(s["narrow_products"], 1)
            act.activation(narrow_f[0:8, :], ps[0:8, 6, :], ACT.Copy).then_inc(s["narrow_copied"], 1)
            split(4)
            for t in range(NT):
                act.wait_ge(s["products"], 6 + t + 1)
                act.activation(zt[:, t, :], ps[:, t, :], ACT.Silu)
            act.wait_ge(s["narrow_products"], 2)
            act.activation(dt_raw[:, :].rearrange("p (t n) -> p t n", t=NT),
                           ps[:, 7, 0:P].rearrange("p (t n) -> p t n", t=NT)[:, :, 0:8], ACT.Copy)
            barrier()
            load((taps[:, :, 0:6], per_feature("conv_w", 0)),
                 (tap_bias[:, 0:6], per_feature("conv_b", 0)),
                 (head_in[:, 0, :], A["dt_bias"][0].partition_broadcast(P)),
                 (head_in[:, 1, :], A["a_log"][0].partition_broadcast(P)),
                 (head_in[:, 2, :], A["d_skip"][0].partition_broadcast(P)),
                 (norm_w[:, :], per_feature("ssd_norm_w", 0)))
            attention(UNITS1, width1, sc1, pt1, by_head=True)
            act.wait_ge(s["params_landed"], 16 * 6)
            split(1)
            barrier()
            for c in range(6):
                act.activation(xc1[:, c, :], pf[:, 8 + c, :], ACT.Identity, scale=taps[:, 3, c:c + 1],
                               bias=tap_bias[:, c:c + 1]).then_inc(s["taps0"], 1)
            act.activation(head_in[:, 3, :], head_in[:, 1, :], ACT.Exp).then_inc(s["gate_exp"], 1)
            softplus(sp[:, 2, :], sp[:, 1, :], sp[:, 4, :], sp[:, 3, :])
            for c in range(6):
                act.wait_ge(s["convolved"], c + 1)
                act.activation(xc1[:, c, :], xc1[:, c, :], ACT.Silu).then_inc(s["activated"], 1)
            for c in range(4):
                act.wait_ge(s["transposed"], c + 1)
                act.activation(xt1[:, :, c * P:c * P + P], ps[:, c, :].rearrange("p (t n) -> p t n", t=NT),
                               ACT.Copy).then_inc(s["tokens_x"], 1)
            act.wait_ge(s["transposed"], 5)
            act.activation(bt1[:, :, :], ps[:, 4, :].rearrange("p (t n) -> p t n", t=NT), ACT.Copy)
            act.wait_ge(s["decay_in"], 1)
            act.activation(dec[:, 4, :], dec[:, 0, :], ACT.Exp).then_inc(s["decays"], 1)
            act.activation(dec[:, 5, :], dec[:, 3, :], ACT.Exp).then_inc(s["decays"], 1)
            act.activation(dec_t[:, :], dec[:, 2, :], ACT.Exp).then_inc(s["decays"], 1)
            barrier()
            for j in range(2 * NT):
                act.wait_ge(s["decay_masked"], j + 1)
                for h in range(4):
                    col = (j // 2) * 8 + (j % 2) * 4 + h
                    act.activation(lm[:, j % 2, h, :], lm[:, j % 2, h, :], ACT.Exp, bias=dec[:, 1, col:col + 1])\
                       .then_inc(s["decay_exp"], 1)
            act.wait_ge(s["variance"], 1)
            act.activation(dev[:, :], mv[:, :, 0], ACT.Sqrt).then_inc(s["deviation"], 1)
            barrier()
            high_parts(oh1, affine=lambda k: (1.0, 0.0) if k < 4 else (norm_w[:, k - 4:k - 3], 0.0))
            barrier()
            load_norm("ln1_g", "ln1_b", 0)
            load((route_b[:, :], A["b_route"][0].partition_broadcast(P)))
            split(KD - TAIL)
            normalise_tiles()
            act.wait_ge(s["params_landed"], 16 * 5)
            split(TAIL)
            norm_high_parts()
            act.wait_ge(s["narrow_products"], 1)
            act.activation(narrow_f[:, :], ps[0:20, 0, :], ACT.Copy).then_inc(s["narrow_copied"], 1)
            split(N_FIRST + RING - slab.n)
            act.wait_ge(s["narrow_products"], 2)
            act.activation(rt[:, :, 0:20], ps[:, 7, 0:P].rearrange("p (t n) -> p t n", t=NT)[:, :, 0:20], ACT.Copy)\
               .then_inc(s["evacuated"], 1)
            act.wait_ge(s["gate_in"], 1)
            act.activation(rt[:, :, 24:28], rt[:, :, 24:28], ACT.Exp).then_inc(s["gate_exp"], 1)
            act.wait_ge(s["gate_in"], 2)
            act.activation(rt[:, :, 52:53], rt[:, :, 52:53], ACT.Exp).then_inc(s["gate_exp"], 1)

            def expert(e, after):
                for c in range(2):
                    act.wait_ge(s["gates_full"], 2 * e + (c + 1))
                    act.activation(esg[:, c, :], ps[:, c, :], ACT.Silu).then_inc(s["silu_done"], 1)
                split(3)
                for c in range(2):
                    act.wait_ge(s["hidden"], 2 * e + (c + 1))
                    act.activation(eh[:, c, :], ehd[:, c, :], ACT.Copy).then_inc(s["hidden_hi"], 1)
                split(after)

            with act.Fori(0, EXPERTS - 1) as e:
                slab.enter(e * N_EXPERT, e * (N_EXPERT // RING))
                expert(e, 3)
            slab.leave()
            slab.n += (EXPERTS - 2) * N_EXPERT
            expert(EXPERTS - 1, 0)
            assert slab.n == L_BASE, slab.n
            load_norm("ln2_g", "ln2_b", 0)
            act.wait_ge(s["params_landed"], 16 * 9)
            barrier()
            normalise_tiles()

            with act.Fori(0, LAYERS) as l:
                slab.enter(l * N_LAYER, l * (N_LAYER // RING))
                end = slab.n + N_LAYER
                split(RING)
                load((taps[:, :, :], per_feature("conv_w_2", l)),
                     (tap_bias[:, :], per_feature("conv_b_2", l)),
                     (gate_bias[:, 0, :], per_feature("b_rg_2", l)),
                     (gate_bias[:, 1, :], per_feature("b_ig_2", l)),
                     (lam[:, 0, :], per_feature("lru_lambda_2", l)),
                     (sink[:, :], A["sinks_2"][l].partition_broadcast(P)))
                norm_high_parts()
                act.wait_ge(s["params_landed"], 16 * 6)
                softplus(lam[:, 2, :], lam[:, 1, :], lam[:, 4, :], lam[:, 3, :])
                for j in range(10):
                    act.wait_ge(s["products"], NT + j + 1)
                    dst = qf[:, j - 2, :] if j >= 2 else (kr[:, :] if j == 0 else vr[:, :])
                    act.activation(dst, ps[:, (j % 6), :], ACT.Copy).then_inc(s["evacuated"], 1)
                    if j % 2:
                        split(2)
                for x in range(len(UNITS2) + 4):
                    if x < len(UNITS2):
                        w = width2(UNITS2[x])
                        act.wait_ge(s["maxima"], x + 1)
                        for h in range(2):
                            act.activation(sc2[:, x % 4, h, 0:w + 1], sc2[:, x % 4, h, 0:w + 1], ACT.Exp,
                                           bias=nmax[:, x % 4, h:h + 1], accum_out=den[:, x % 4, h:h + 1])\
                               .then_inc(s["probs"], 1)
                    u = x - 1
                    if 0 <= u < len(UNITS2):
                        w = width2(UNITS2[u])
                        act.wait_ge(s["sums_inverted"], u + 1)
                        act.activation(sc2[:, u % 4, 1, 0:w], sc2[:, u % 4, 1, 0:w], ACT.Copy,
                                       scale=rden[:, u % 4, 1:2]).then_inc(s["divided_too"], 1)
                    u = x - 2
                    if 0 <= u < len(UNITS2):
                        w = width2(UNITS2[u])
                        act.wait_ge(s["probs_t"], u + 1)
                        if u >= 2:
                            act.wait_ge(s["values"], u - 1)
                        src = ps[:, 4 + u % 2, :].rearrange("p (h n) -> p h n", h=2)
                        act.activation(pt2[:, u % 2, :, 0:w], src[:, :, 0:w], ACT.Copy)\
                           .then_inc(s["probs_t_copied"], 1)
                    u = x - 4
                    if u >= 0:
                        i, p = UNITS2[u]
                        act.wait_ge(s["values"], u + 1)
                        act.activation(oh2[:, p, i * P:i * P + P], ps[:, 6 + u % 2, 0:P], ACT.Copy)\
                           .then_inc(s["hi_ready"], 1)
                barrier()

                def gates_of(p, products):
                    b = 4 * (p % 2)
                    for c in range(2):
                        if products is not None:
                            act.wait_ge(s["products"], products + c + 1)
                        if p >= 1:
                            act.wait_ge(s["banks_read"], 2 * (p - 1) + c + 1)
                        act.activation(sgm[:, c, :], ps[:, b + c, :], ACT.Sigmoid).then_inc(s["evacuated"], 1)

                for p in range(4):
                    gates_of(p, 4 * p)
                    split(4)
                barrier()
                for j in range(8):
                    act.wait_ge(s["products"], j + 1)
                    if j >= 4:
                        act.wait_ge(s["convolved"], j - 3)
                    link(act.activation(t4[:, j % 4, :], ps[:, j, :], ACT.Copy))
                    act.activation(xc2[:, j, :], t4[:, j % 4, :], ACT.Identity, scale=taps[:, 3, j:j + 1],
                                   bias=tap_bias[:, j:j + 1]).then_inc(s["taps0"], 1)
                    if j % 2:
                        split(2)
                        for i in ((j - 3, j - 2) if j >= 3 else ()):
                            act.wait_ge(s["convolved"], i + 1)
                            act.activation(yh[:, i, :], xc2[:, i, :], ACT.Copy).then_inc(s["hi_ready"], 1)
                for i in (6, 7):
                    act.wait_ge(s["convolved"], i + 1)
                    act.activation(yh[:, i, :], xc2[:, i, :], ACT.Copy).then_inc(s["hi_ready"], 1)
                for j in range(8):
                    act.wait_ge(s["products"], 8 + j + 1)
                    act.activation(ga[:, j, :], ps[:, j, :], ACT.Sigmoid, bias=gate_bias[:, 0, j:j + 1])\
                       .then_inc(s["r_done"], 1)
                    if j % 4 == 3:
                        split(1)
                for j in range(8):
                    act.wait_ge(s["products"], 16 + j + 1)
                    if j >= 2:
                        act.wait_ge(s["i_used"], j - 1)
                    act.activation(vbuf[:, j % 2, :], ps[:, j, :], ACT.Sigmoid, bias=gate_bias[:, 1, j:j + 1])\
                       .then_inc(s["i_done"], 1)
                    if j % 4 == 3:
                        split(1)
                for j in range(8):
                    act.activation(t8[:, j, :], ga[:, j, :], ACT.Tanh, scale=lam[:, 6, j:j + 1])\
                       .then_inc(s["tanh_done"], 1)
                act.wait_ge(s["tanh_done"], 8)
                for j in range(8):
                    act.activation(ga[:, j, :], ga[:, j, :], ACT.Exp, scale=lam[:, 7, j:j + 1])\
                       .then_inc(s["decay_done"], 1)
                split(2)
                for j in range(8):
                    act.wait_ge(s["mult2"], j + 1)
                    act.activation(t8[:, j, :], t8[:, j, :], ACT.Sqrt).then_inc(s["mult"], 1)
                for p in range(4):
                    for j in (2 * p, 2 * p + 1):
                        act.wait_ge(s["products"], 24 + j + 1)
                        act.activation(gg[:, j, :], ps[:, j, :], ACT.Gelu_apprx_tanh).then_inc(s["gelu_done"], 1)
                    if p:
                        split(2)
                for j in range(8):
                    act.wait_ge(s["chunk_ready"], j + 1)
                    act.activation(yh[:, j, :], xc2[:, j, :], ACT.Copy).then_inc(s["hi_ready"], 1)
                    if j in (2, 5):
                        split(2)
                barrier()
                for p in range(4):
                    gates_of(p, 4 * p - 4 if p >= 2 else None)
                    split(2)
                    for j in (2 * p, 2 * p + 1):
                        act.wait_ge(s["chunk_ready"], j + 1)
                        act.activation(mh[:, j, :], mg[:, j, :], ACT.Copy).then_inc(s["hi_ready"], 1)
                    if p >= 2:
                        split(2)
                barrier()
                load_norm("ln1_g_2", "ln1_b_2", l)
                load((mt[:, :, :], A["mem_2"][0].rearrange("(t p) d -> p t d", p=P)))
                split(KD - TAIL)
                normalise_tiles()
                act.wait_ge(s["params_landed"], 16 * 5)
                split(TAIL)
                norm_high_parts()
                for j in range(8):
                    act.wait_ge(s["products"], NT + j + 1)
                    act.activation(qc[:, j, :], ps[:, j, :], ACT.Copy).then_inc(s["evacuated"], 1)
                    if j % 2:
                        split(2)
                high_parts(mem_h, nt=MEM, base=KD)
                for j in range(8):
                    if j % 2 == 0:
                        split(1)
                    act.wait_ge(s["products"], NT + 8 + j + 1)
                    act.activation(kc[:, j, :], ps[:, j, 0:MEM], ACT.Copy).then_inc(s["evacuated"], 1)
                    if j % 2:
                        split(1)
                split(8)
                for t in range(2):
                    act.wait_ge(s["products"], NT + 16 + t + 1)
                    act.activation(vc[:, t, :].rearrange("p (h n) -> p h n", h=2), ps[:, 2 * t:2 * t + 2, :], ACT.Copy)
                barrier()
                attention(UNITS3, width3, sc3, pt3)
                load_norm("ln2_g_2", "ln2_b_2", l)
                high_parts(oh3)
                split(KD - TAIL)
                normalise_tiles()
                act.wait_ge(s["params_landed"], 16 * 4)
                split(TAIL)
                norm_high_parts(base=KD)
                pairs = 0
                for half, (c0, n) in enumerate(FF_HALVES):
                    for p in range(n // 2):
                        b = 4 * (pairs % 2)
                        for c in range(2):
                            act.wait_ge(s["gates_full"], 2 * pairs + c + 1)
                            if pairs >= 2:
                                act.wait_ge(s["hidden"], 2 * (pairs - 2) + c + 1)
                            act.activation(fsg[:, pairs % 2, c, :], ps[:, b + c, :], ACT.Silu)\
                               .then_inc(s["silu_done"], 1)
                        split(2)
                        for c in range(2):
                            act.wait_ge(s["hidden"], 2 * pairs + c + 1)
                            act.activation(fh[:, 2 * p + c, :], fhd[:, c, :], ACT.Copy).then_inc(s["hidden_hi"], 1)
                        split(2)
                        pairs += 1
                    if half == 0:
                        load_norm("ln3_g_2", "ln3_b_2", l)
                        split(n)
                act.wait_ge(s["params_landed"], 16 * 8)
                barrier()
                split(FF_HALVES[1][1] - RING)
                normalise_tiles()
                assert slab.n == end

        @block.vector
        def _(dve):
            phase = Count()
            links = [0]

            def link(ins):
                links[0] += 1
                ins.then_inc(s["dve_link"], 1)
                dve.wait_ge(s["dve_link"], links[0])

            def barrier():
                dve.wait_ge(arrived, 2)
                dve.drain()
                dve.sem_clear(phase_range)
                dve.sem_clear(arrived)
                dve.sem_clear(go[1 - phase.n % 2])
                dve.drain().then_inc(go[phase.n % 2], 1)
                phase.n += 1
                links[0] = 0

            def low_parts(hi, lo, source, nt=T, base=0):
                for k in range(KD):
                    dve.wait_ge(s["hi_ready"], base + k + 1)
                    dve.tensor_tensor(lo[:, k, 0:nt], source(k), hi[:, k, 0:nt].bitcast(F32), ALU.subtract)\
                       .then_inc(s["lo_ready"], 1)

            def from_banks(nt=T):
                return lambda k: ps[:, k, 0:nt]

            def from_vbuf(k):
                return vbuf[:, k % 2, :]

            def heads(v, n):
                return v.rearrange("p (h n) -> p h n", h=n)

            def wide(v, n):
                return v.unsqueeze(2).broadcast_to([v.shape[0], v.shape[1], n])

            def attention(units, width, sc, mask_of, scale, out_of, by_head=False):
                def front(u):
                    unit = units[u]
                    w, high = width(unit), nmax[:, u % 4, :]
                    dve.wait_ge(s["scores"], u + 1)
                    if u >= 2:
                        dve.wait_ge(s["probs_t"], 2 * (u - 1) if by_head else u - 1)
                    dst, src = sc[:, u % 2, :, 0:w], ps[:, 2 * (u % 2):2 * (u % 2) + 2, 0:w]
                    mask = mask_of(unit)
                    if mask is None:
                        dve.tensor_scalar(dst, src, scale, None, ALU.mult).then_inc(s["scores_read"], 1)
                    else:
                        dve.scalar_tensor_tensor(dst, src, scale, mask.unsqueeze(1).broadcast_to([P, 2, w]),
                                                 ALU.mult, ALU.add).then_inc(s["scores_read"], 1)
                    dve.wait_ge(s["scores_read"], u + 1)
                    dve.tensor_reduce(high, dst, AX.X, ALU.max, negate=True).then_inc(s["maxima"], 1)

                def finish(u):
                    dst, total = out_of(units[u]), den[:, u % 4, :]
                    dv = dst.shape[2]
                    dve.wait_ge(s["values"], u + 1)
                    link(dve.reciprocal(rden[:, u % 4, :], total))
                    dve.tensor_tensor(dst, heads(values_bank(u)[:, 0:2 * dv], 2),
                                      wide(rden[:, u % 4, :], dv), ALU.mult).then_inc(s["values_read"], 1)

                for u in range(len(units)):
                    front(u)
                    if u >= 3:
                        finish(u - 3)
                for u in range(len(units) - 3, len(units)):
                    finish(u)

            def softplus_start(x, mag):
                link(dve.tensor_scalar(mag, x, -1.0, None, ALU.mult))
                dve.tensor_tensor(mag, mag, x, ALU.max).then_inc(s["sp_in"], 1)

            def softplus_end(x, e, u, log, tmp, to):
                dve.wait_ge(s["sp_exp"], 1)
                dve.tensor_scalar(u, e, 1.0, None, ALU.add).then_inc(s["sp_sum"], 1)
                dve.wait_ge(s["sp_sum"], 1)
                link(dve.tensor_scalar(tmp, u, -1.0, None, ALU.add))
                link(dve.tensor_tensor(tmp, e, tmp, ALU.subtract))
                link(dve.reciprocal(to, u))
                link(dve.tensor_tensor(tmp, tmp, to, ALU.mult))
                dve.wait_ge(s["sp_log"], 1)
                link(dve.tensor_tensor(tmp, tmp, log, ALU.add))
                link(dve.tensor_scalar(to, x, 0.0, None, ALU.max))
                link(dve.tensor_tensor(to, to, tmp, ALU.add))

            def layer_norm(alpha, in_banks=True):
                def first(t):
                    if in_banks:
                        dve.wait_ge(s["products"], t + 1)
                        y = res[:, t, :].rearrange("p (a b) -> p a b", a=2)
                        dve.scalar_tensor_tensor(y, y, alpha, ps[:, 2 * t:2 * t + 2, :], ALU.mult, ALU.add)\
                           .then_inc(s["summed"], 1)
                        dve.wait_ge(s["summed"], t + 1)
                    dve.bn_stats(stats[:, t, 0, :], res[:, t, 0:512])
                    link(dve.bn_stats(stats[:, t, 1, :], res[:, t, 512:D]))
                    link(dve.bn_aggr(mv[:, t, :], stats[:, t, :, :]))
                    dve.tensor_scalar(mv[:, t, 1:2], mv[:, t, 1:2], EPS, None, ALU.add).then_inc(s["variance"], 1)

                def second(t):
                    dve.wait_ge(s["deviation"], t + 1)
                    link(dve.reciprocal(rdev[:, t:t + 1], dev[:, t:t + 1]))
                    if t == NT - 1:
                        dve.wait_ge(s["normalised"], t)
                        dve.tensor_scalar(res[:, t, :], res[:, t, :], mv[:, t, 0:1], rdev[:, t:t + 1],
                                          ALU.subtract, ALU.mult).then_inc(s["normalised"], 1)
                        return
                    dve.scalar_tensor_tensor(shift[:, t:t + 1], mv[:, t, 0:1], -1.0, rdev[:, t:t + 1], ALU.mult,
                                             ALU.mult).then_inc(s["shift_ready"], 1)

                first(0)
                for t in range(1, NT):
                    first(t)
                    second(t - 1)
                second(NT - 1)

            def residual_gain(scale=None):
                for t in range(NT):
                    ins = dve.tensor_tensor(res[:, t, :], res[:, t, :], gain[:, 0, :], ALU.mult)
                link(ins)
                for t in range(NT):
                    ins = dve.tensor_tensor(res[:, t, :], res[:, t, :], gain[:, 1, :], ALU.add)
                link(ins)
                if scale is not None:
                    link(dve.tensor_scalar(res[:, :, :], res[:, :, :], scale, None, ALU.mult))

            low_parts(x_hi, x_lo, from_banks())
            barrier()
            for v in (kz, iz):
                dve.memset(v[:, :, :], 0.0)
            barrier()
            cos, sin = consts["cos1"], consts["sin1"]
            for j, c in enumerate((0, 1, 2, 3, 5, 6)):
                dve.wait_ge(s["products"], j + 1)
                dve.tensor_tensor(rl[:, 0, :], ps[:, j, :], sin, ALU.mult).then_inc(s["banks_read"], 1)
                link(dve.tensor_tensor(rl[:, 1, :], pf[:, c, :], cos, ALU.mult))
                dve.wait_ge(s["banks_read"], j + 1)
                link(dve.tensor_tensor(pf[:, c, :], rl[:, 0, :], rl[:, 1, :], ALU.add))
            for c, plain, turned, ready in ((4, 6, 7, 11), (7, 0, 1, 12)):
                dve.wait_ge(s["products"], ready)
                link(dve.tensor_tensor(rl[:, 0, :], ps[:, turned, :], sin, ALU.mult))
                link(dve.tensor_tensor(rl[:, 1, :], ps[:, plain, :], cos, ALU.mult))
                for h, half in enumerate((slice(0, HD), slice(HD, P))):
                    ins = dve.tensor_tensor((kz if c == 4 else iz)[half, h, :], rl[half, 0, :], rl[half, 1, :], ALU.add)
                link(ins)
            barrier()
            link(dve.memset(ones[:, :], 1.0))
            for i in range(1, NT):
                w = (i + 1) * P
                for h in range(I_HEADS):
                    n = 4 * (i - 1) + h + 1
                    dve.wait_ge(s["relu"], n)
                    if h == 0:
                        dve.tensor_scalar(ix[:, i - 1, 0:w], rl[:, h, 0:w], iw[:, i, h:h + 1], None, ALU.mult)\
                           .then_inc(s["relu_used"], 1)
                    else:
                        dve.scalar_tensor_tensor(ix[:, i - 1, 0:w], rl[:, h, 0:w], iw[:, i, h:h + 1],
                                                 ix[:, i - 1, 0:w], ALU.mult, ALU.add).then_inc(s["relu_used"], 1)
                    dve.wait_ge(s["relu_used"], n)
                link(dve.tensor_tensor(ix[:, i - 1, w - P:w], ix[:, i - 1, w - P:w], consts["cmask"], ALU.add))
            link(dve.tensor_copy(mb[:, 0, 0:P], consts["cmask"]))
            for i in range(1, NT):
                w = (i + 1) * P
                sc, work, eq, pre = ix[:, i - 1, 0:w], ix[:, 3, 0:w], rl[:, 0, 0:w], rl[:, 1, 0:w]
                for r in range(TOPK // 8):
                    link(dve.max(top8[:, :], sc if r == 0 else work))
                    if r < TOPK // 8 - 1:
                        link(dve.match_replace(work, top8[:, :], sc if r == 0 else work, GONE))
                least = top8[:, 7:8]
                link(dve.tensor_scalar(mb[:, i, 0:w], sc, least, None, ALU.is_gt))
                link(dve.tensor_reduce(short[:, :], mb[:, i, 0:w], AX.X, ALU.add))
                link(dve.tensor_scalar(short[:, :], short[:, :], -1.0, float(TOPK), ALU.mult, ALU.add))
                link(dve.tensor_scalar(eq, sc, least, None, ALU.is_equal))
                link(dve.tensor_tensor_scan(pre, ones[:, 0:w], eq, 0.0, ALU.mult, ALU.add))
                link(dve.scalar_tensor_tensor(eq, pre, short[:, 0:1], eq, ALU.is_le, ALU.mult))
                link(dve.tensor_tensor(mb[:, i, 0:w], mb[:, i, 0:w], eq, ALU.add))
                link(dve.tensor_scalar(mb[:, i, 0:w], mb[:, i, 0:w], -1.0, -NEG, ALU.add, ALU.mult))
            barrier()
            attention(UNITS1, width1, sc1, lambda unit: mb[:, unit[0], 0:width1(unit)], HD ** -0.5,
                      lambda unit: heads(ot1[:, unit[0], P * unit[1]:P * unit[1] + P], 2), by_head=True)
            barrier()
            x_sp, mag, e_sp, u_sp, l_sp, tmp, dt = (sp[:, i, :] for i in range(7))
            link(dve.tensor_tensor(x_sp.rearrange("p (t h) -> p t h", t=NT), dt_raw[:, :].rearrange("p (t h) -> p t h", t=NT),
                                   head_in[:, 0:1, :].broadcast_to([P, NT, 8]), ALU.add))
            softplus_start(x_sp, mag)
            for c in range(6):
                dve.wait_ge(s["taps0"], c + 1)
                for back in (1, 2, 3):
                    ins = dve.scalar_tensor_tensor(xc1[:, c, back:T], pf[:, 8 + c, 0:T - back], taps[:, 3 - back, c:c + 1],
                                                   xc1[:, c, back:T], ALU.mult, ALU.add)
                    if back < 3:
                        link(ins)
                ins.then_inc(s["convolved"], 1)
            softplus_end(x_sp, e_sp, u_sp, l_sp, tmp, dt)
            dve.wait_ge(s["gate_exp"], 1)
            link(dve.tensor_tensor(dt_a[:, :].rearrange("p (t h) -> p t h", t=NT), dt.rearrange("p (t h) -> p t h", t=NT),
                                   head_in[:, 3:4, :].broadcast_to([P, NT, 8]), ALU.mult))
            dve.tensor_scalar(dt_a[:, :], dt_a[:, :], -1.0, None, ALU.mult).then_inc(s["sp_done"], 1)
            dve.wait_ge(s["cumulated"], 1)
            link(dve.tensor_copy(dec[:, 0, :], ps[:, 5, 0:32]))
            link(dve.tensor_copy(dec[:, 2, :], ps[:, 6, 0:32]))
            link(dve.tensor_scalar(dec[:, 1, :], dec[:, 0, :], -1.0, None, ALU.mult))
            dve.tensor_tensor(dec[:, 3, :], dec[:, 2, :], dec[:, 0, :], ALU.subtract).then_inc(s["decay_in"], 1)
            dve.wait_ge(s["tokens_x"], 4)
            x3, xdt3, xdec3 = (v[:, :, :].rearrange("p t (h n) -> p (t h) n", n=HD) for v in (xt1, xdt, xdec))
            link(dve.tensor_tensor(xdt3, x3, wide(dt, HD), ALU.mult))
            for t in range(NT):
                dve.tensor_tensor(heads(xsk[:, t, :], 8), heads(xt1[:, t, :], 8), wide(head_in[:, 2, :], HD), ALU.mult)
            dve.wait_ge(s["decays"], 3)
            dve.tensor_tensor(xdec3, xdt3, wide(dec[:, 5, :], HD), ALU.mult)
            dve.memset(prev[:, :], 0.0)
            dt3 = dec_t[:, :].rearrange("p (t h) -> p t h", t=NT)
            for g in range(S_GROUPS):
                r = slice(HD * g, HD * g + HD)
                dve.tensor_copy(dec4[r, :, :], dt3[r, :, 4 * g:4 * g + 4])
            dve.memset(cz[HD:P, 0, :], 0.0)
            dve.memset(cz[0:HD, 1, :], 0.0)
            dve.wait_ge(s["activated"], 6)
            dve.tensor_copy(cz[0:HD, 0, :], xc1[0:HD, 5, :])
            dve.tensor_copy(cz[HD:P, 1, :], xc1[HD:P, 5, :])
            barrier()
            for c in range(NT):
                for g in range(S_GROUPS):
                    j = 2 * c + g
                    dve.wait_ge(s["cb_products"], j + 1)
                    if c >= 1 and g == 0:
                        dve.wait_ge(s["chunk_products"], c)
                    dve.tensor_tensor(lm[:, g, :, :], heads(ps[:, 2 + g, :], 4),
                                      consts["cmask_t"].unsqueeze(1).broadcast_to([P, 4, P]), ALU.add)\
                       .then_inc(s["decay_masked"], 1)
                for g in range(S_GROUPS):
                    j = 2 * c + g
                    dve.wait_ge(s["decay_exp"], 4 * (j + 1))
                    dve.tensor_tensor(lm[:, g, :, :], lm[:, g, :, :],
                                      ps[:, g, 0:P].unsqueeze(1).broadcast_to([P, 4, P]), ALU.mult)\
                       .then_inc(s["decayed"], 1)
                dve.wait_ge(s["chunk_products"], c + 1)
                for g in range(S_GROUPS):
                    ins = dve.tensor_tensor(heads(yt[:, 256 * g:256 * g + 256], 4), heads(ps[:, 5 + 2 * g, 0:256], 4),
                                            wide(dec[:, 4, 8 * c + 4 * g:8 * c + 4 * g + 4], HD), ALU.mult)
                link(ins)
                link(dve.tensor_tensor(yt[:, :], yt[:, :], ps[:, 4, :], ALU.add))
                link(dve.tensor_tensor(heads(prev[:, :], 4), heads(prev[:, :], 4), wide(dec4[:, c, :], HD), ALU.mult))
                dve.tensor_tensor(prev[:, :], prev[:, :], ps[:, 6, 0:256], ALU.add).then_inc(s["state_ready"], 1)
                dve.wait_ge(s["state_ready"], c + 1)
                link(dve.tensor_tensor(yt[:, :], yt[:, :], xsk[:, c, :], ALU.add))
                link(dve.tensor_tensor(ot1[:, c, 512:D], yt[:, :], zt[:, c, :], ALU.mult))
                link(dve.scalar_tensor_tensor(sq[:, :], ot1[:, c, 512:D], 1.0, ot1[:, c, 512:D], ALU.mult, ALU.mult,
                                              accum_out=mv[:, c, 0:1]))
            dve.tensor_scalar(mv[:, :, 0], mv[:, :, 0], 1.0 / 512, EPS, ALU.mult, ALU.add).then_inc(s["variance"], 1)
            dve.wait_ge(s["deviation"], 1)
            link(dve.reciprocal(rdev[:, :], dev[:, :]))
            for c in range(NT):
                dve.tensor_scalar(ot1[:, c, 512:D], ot1[:, c, 512:D], rdev[:, c:c + 1], None, ALU.mult)
            barrier()
            low_parts(oh1, ol1, from_vbuf)
            barrier()
            layer_norm(ALPHA1)
            low_parts(x_hi, x_lo, from_vbuf)
            dve.wait_ge(s["evacuated"], 1)
            link(dve.tensor_tensor(rt[:, :, 0:20], rt[:, :, 0:20],
                                   route_b[:, :].unsqueeze(1).broadcast_to([P, NT, 20]), ALU.add))
            one4 = lambda v, n: v.broadcast_to([P, NT, n])

            def first_of_best(logits, best, onehot):
                link(dve.tensor_reduce(best, logits, AX.X, ALU.max))
                link(dve.tensor_tensor(onehot, logits, one4(best, 4), ALU.is_equal))
                link(dve.tensor_tensor(onehot, onehot, rank, ALU.mult))
                link(dve.tensor_reduce(rt[:, :, 63:64], onehot, AX.X, ALU.max))
                link(dve.tensor_tensor(onehot, rank, one4(rt[:, :, 63:64], 4), ALU.is_equal))

            rank = rt[:, :, 56:60]
            for j in range(4):
                link(dve.memset(rt[:, :, 56 + j:57 + j], float(4 - j)))
            g_log, g_max, g_hot, g_exp = rt[:, :, 0:4], rt[:, :, 20:21], rt[:, :, 28:32], rt[:, :, 24:28]
            first_of_best(g_log, g_max, g_hot)
            dve.tensor_tensor(g_exp, g_log, one4(g_max, 4), ALU.subtract).then_inc(s["gate_in"], 1)
            e_log, e_tmp = rt[:, :, 32:36], rt[:, :, 36:40]
            link(dve.tensor_tensor(e_log, rt[:, :, 4:8], one4(rt[:, :, 28:29], 4), ALU.mult))
            for g in range(1, GROUPS):
                link(dve.tensor_tensor(e_tmp, rt[:, :, 4 + 4 * g:8 + 4 * g], one4(rt[:, :, 28 + g:29 + g], 4), ALU.mult))
                link(dve.tensor_tensor(e_log, e_log, e_tmp, ALU.add))
            m1, m2, hot1, hot2, e12 = rt[:, :, 21:22], rt[:, :, 22:23], rt[:, :, 40:44], rt[:, :, 44:48], rt[:, :, 52:53]
            first_of_best(e_log, m1, hot1)
            link(dve.tensor_scalar(e_tmp, hot1, NEG, None, ALU.mult))
            link(dve.tensor_tensor(e_tmp, e_tmp, e_log, ALU.add))
            first_of_best(e_tmp, m2, hot2)
            dve.tensor_tensor(e12, m2, m1, ALU.subtract).then_inc(s["gate_in"], 1)
            dve.wait_ge(s["gate_exp"], 2)
            gsum, w1, w2 = rt[:, :, 53:54], rt[:, :, 54:55], rt[:, :, 55:56]
            link(dve.tensor_reduce(gsum, g_exp, AX.X, ALU.add))
            link(dve.tensor_scalar(w1, e12, 1.0, None, ALU.add))
            link(dve.tensor_tensor(w1, w1, gsum, ALU.mult))
            link(dve.reciprocal(w1, w1))
            link(dve.tensor_tensor(w2, w1, e12, ALU.mult))
            link(dve.tensor_tensor(hot1, hot1, one4(w1, 4), ALU.mult))
            link(dve.tensor_tensor(hot2, hot2, one4(w2, 4), ALU.mult))
            link(dve.tensor_tensor(hot1, hot1, hot2, ALU.add))
            for g in range(GROUPS):
                link(dve.tensor_tensor(gates[:, :, 4 * g:4 * g + 4], hot1, one4(rt[:, :, 28 + g:29 + g], 4), ALU.mult))

            def expert_hidden(e):
                for c in range(2):
                    dve.wait_ge(s["silu_done"], 2 * e + (c + 1))
                    dve.wait_ge(s["ups_full"], 2 * e + (c + 1))
                    dve.tensor_tensor(ehd[:, c, :], esg[:, c, :], ps[:, 2 + c, :], ALU.mult).then_inc(s["hidden"], 1)
                for c in range(2):
                    dve.wait_ge(s["hidden_hi"], 2 * e + (c + 1))
                    dve.tensor_tensor(el[:, c, :], ehd[:, c, :], eh[:, c, :].bitcast(F32), ALU.subtract)\
                       .then_inc(s["hidden_lo"], 1)

            def expert_sum(e):
                for half in range(2):
                    for t in range(NT):
                        dve.wait_ge(s["downs_full"], 8 * e + (4 * half + t + 1))
                        y = res[:, t, 512 * half:512 * half + 512]
                        gate = gates[:, t, bass.ds(e, 1)]
                        dve.scalar_tensor_tensor(y, ps[:, 4 + t, :], gate, y, ALU.mult, ALU.add)\
                           .then_inc(s["downs_free"], 1)

            expert_hidden(0)
            residual_gain(ALPHA1)
            with dve.Fori(0, EXPERTS - 1) as e:
                expert_sum(e)
                expert_hidden(e + 1)
            expert_sum(EXPERTS - 1)
            barrier()
            layer_norm(1.0, in_banks=False)
            norm_links = links[0]

            with dve.Fori(0, LAYERS) as l:
                low_parts(x_hi, x_lo, from_vbuf)
                dve.wait_ge(s["params_landed"], 16 * 6)
                link(dve.tensor_scalar(lam[:, 0, :], lam[:, 0, :], -1.0, None, ALU.mult))
                softplus_start(lam[:, 0, :], lam[:, 1, :])
                softplus_end(lam[:, 0, :], lam[:, 2, :], lam[:, 3, :], lam[:, 4, :], lam[:, 5, :], lam[:, 6, :])
                link(dve.tensor_scalar(lam[:, 7, :], lam[:, 6, :], -8.0, None, ALU.mult))
                link(dve.tensor_scalar(lam[:, 6, :], lam[:, 6, :], 8.0, None, ALU.mult))
                turned = [0]

                def turn(n, raw, dst):
                    dve.wait_ge(s["small_products"], n + 1)
                    dve.tensor_tensor(vbuf[:, 0, :], ps[:, 6 + n % 2, :], consts["sin2"], ALU.mult)\
                       .then_inc(s["banks_read"], 1)
                    link(dve.tensor_tensor(vbuf[:, 1, :], raw, consts["cos2"], ALU.mult))
                    dve.wait_ge(s["banks_read"], n + 1)
                    dve.tensor_tensor(dst, vbuf[:, 0, :], vbuf[:, 1, :], ALU.add).then_inc(s["turned"], 1)
                    turned[0] += 1
                    dve.wait_ge(s["turned"], turned[0])

                lower, upper = slice(0, HD), slice(HD, P)
                for i in range(KV_HEADS2):
                    dve.memset(ks[upper, 2 * i, :], 0.0)
                    dve.memset(ks[lower, 2 * i + 1, :], 0.0)
                turn(0, kr[:, :], kr[:, :])
                dve.tensor_copy(ks[lower, 0, :], kr[lower, :])
                dve.tensor_copy(ks[upper, 3, :], kr[upper, :])
                dve.wait_ge(s["small_products"], 2)
                dve.tensor_copy(vt2[:, :, :], ps[:, 7, :].rearrange("p (t n) -> p t n", t=NT))\
                   .then_inc(s["banks_read"], 1)
                dve.wait_ge(s["small_products"], 3)
                dve.tensor_copy(ks[lower, 2, :], ps[lower, 6, :])
                dve.tensor_copy(ks[upper, 1, :], ps[upper, 6, :]).then_inc(s["banks_read"], 1)
                for c in range(8):
                    turn(3 + c, qf[:, c, :], qf[:, c, :])

                def mask2(unit):
                    return consts["swamask"] if unit[0] else consts["swamask"][:, P:2 * P]

                def front(u):
                    unit = UNITS2[u]
                    w = width2(unit)
                    dve.wait_ge(s["scores"], u + 1)
                    if u >= 4:
                        dve.wait_ge(s["probs_t"], u - 3)
                    q = 2 * unit[1]
                    dve.tensor_copy(sc2[:, u % 4, :, w], sink[:, q:q + 2])
                    dve.scalar_tensor_tensor(sc2[:, u % 4, :, 0:w], ps[:, 2 * (u % 2):2 * (u % 2) + 2, 0:w], HD ** -0.5,
                                             mask2(unit).unsqueeze(1).broadcast_to([P, 2, w]), ALU.mult, ALU.add)\
                       .then_inc(s["scores_read"], 1)
                    dve.wait_ge(s["scores_read"], u + 1)
                    dve.tensor_reduce(nmax[:, u % 4, :], sc2[:, u % 4, :, 0:w + 1], AX.X, ALU.max, negate=True)\
                       .then_inc(s["maxima"], 1)

                def divide(u):
                    dve.wait_ge(s["probs"], 2 * u + 2)
                    dve.reciprocal(rden[:, u % 4, :], den[:, u % 4, :]).then_inc(s["sums_inverted"], 1)
                    dve.wait_ge(s["sums_inverted"], u + 1)
                    w = width2(UNITS2[u])
                    dve.tensor_scalar(sc2[:, u % 4, 0, 0:w], sc2[:, u % 4, 0, 0:w], rden[:, u % 4, 0:1], None, ALU.mult)\
                       .then_inc(s["divided"], 1)

                def low_part(u):
                    i, p = UNITS2[u]
                    dve.wait_ge(s["hi_ready"], KD + u + 1)
                    dve.tensor_tensor(ol2[:, p, i * P:i * P + P], ps[:, 6 + u % 2, 0:P],
                                      oh2[:, p, i * P:i * P + P].bitcast(F32), ALU.subtract).then_inc(s["values_read"], 1)

                n = len(UNITS2)
                for u in range(n + 5):
                    if u < n:
                        front(u)
                    if 1 <= u <= n:
                        divide(u - 1)
                    if u >= 5:
                        low_part(u - 5)
                barrier()
                residual_gain()
                for p in range(4):
                    b = 4 * (p % 2)
                    for c in range(2):
                        dve.wait_ge(s["evacuated"], 2 * p + c + 1)
                        dve.wait_ge(s["products"], 4 * p + 2 + c + 1)
                        dve.tensor_tensor(mg[:, 2 * p + c, :], sgm[:, c, :], ps[:, b + 2 + c, :], ALU.mult)\
                           .then_inc(s["banks_read"], 1)
                barrier()
                for j in range(8):
                    dve.wait_ge(s["taps0"], j + 1)
                    for back in (1, 2, 3):
                        ins = dve.scalar_tensor_tensor(xc2[:, j, back:T], t4[:, j % 4, 0:T - back],
                                                       taps[:, 3 - back, j:j + 1], xc2[:, j, back:T], ALU.mult, ALU.add)
                        if back < 3:
                            link(ins)
                    ins.then_inc(s["convolved"], 1)
                low_parts(yh, yl, lambda k: xc2[:, k, :])
                for j in range(8):
                    dve.wait_ge(s["i_done"], j + 1)
                    dve.tensor_tensor(xc2[:, j, :], xc2[:, j, :], vbuf[:, j % 2, :], ALU.mult).then_inc(s["i_used"], 1)
                dve.wait_ge(s["i_used"], 8)
                for j in range(8):
                    dve.wait_ge(s["tanh_done"], j + 1)
                    dve.wait_ge(s["decay_done"], j + 1)
                    if j >= 2:
                        dve.wait_ge(s["mult2"], j - 1)
                    link(dve.tensor_tensor(vbuf[:, j % 2, :], ga[:, j, :], ga[:, j, :], ALU.mult))
                    dve.scalar_tensor_tensor(t8[:, j, :], vbuf[:, j % 2, :], 1.0, t8[:, j, :], ALU.add, ALU.mult)\
                       .then_inc(s["mult2"], 1)

                def low(j):
                    dve.wait_ge(s["hi_ready"], 8 + j + 1)
                    dve.tensor_tensor(yl[:, j, :], xc2[:, j, :], yh[:, j, :].bitcast(F32), ALU.subtract)

                for j in range(8):
                    dve.wait_ge(s["mult"], j + 1)
                    link(dve.tensor_tensor(xc2[:, j, :], xc2[:, j, :], t8[:, j, :], ALU.mult))
                    link(dve.tensor_tensor_scan(t8[:, j, :], ga[:, j, :], xc2[:, j, :], 0.0, ALU.mult, ALU.add))
                    dve.wait_ge(s["gelu_done"], j + 1)
                    dve.tensor_tensor(xc2[:, j, :], t8[:, j, :], gg[:, j, :], ALU.mult).then_inc(s["chunk_ready"], 1)
                    if j >= 2:
                        low(j - 2)
                low(6)
                low(7)
                barrier()
                for p in range(4):
                    b = 4 * (p % 2)
                    for c in range(2):
                        j = 2 * p + c
                        dve.wait_ge(s["evacuated"], j + 1)
                        dve.wait_ge(s["products"], (4 * p - 2 if p >= 2 else 2 * p) + c + 1)
                        dve.tensor_tensor(vbuf[:, c, :], sgm[:, c, :], ps[:, b + 2 + c, :], ALU.mult)\
                           .then_inc(s["banks_read"], 1)
                        dve.wait_ge(s["banks_read"], j + 1)
                        dve.tensor_tensor(mg[:, j, :], mg[:, j, :], vbuf[:, c, :], ALU.add).then_inc(s["chunk_ready"], 1)
                    for j in (2 * p, 2 * p + 1):
                        dve.wait_ge(s["hi_ready"], j + 1)
                        dve.tensor_tensor(ml[:, j, :], mg[:, j, :], mh[:, j, :].bitcast(F32), ALU.subtract)
                barrier()
                layer_norm(ALPHA2)
                low_parts(x_hi, x_lo, from_vbuf)
                residual_gain()
                low_parts(mem_h, mem_l, from_banks(MEM), nt=MEM, base=KD)
                barrier()
                attention(UNITS3, width3, sc3, lambda unit: None, 256 ** -0.5,
                          lambda unit: heads(ot3[:, unit[0], 512 * unit[1]:512 * unit[1] + 512], 2))
                low_parts(oh3, ol3, from_banks())
                layer_norm(ALPHA2)
                low_parts(x_hi, x_lo, from_vbuf, base=KD)
                residual_gain()
                pairs = 0
                for half, (c0, n) in enumerate(FF_HALVES):
                    for p in range(n // 2):
                        b = 4 * (pairs % 2)
                        for c in range(2):
                            j = 2 * pairs + c
                            dve.wait_ge(s["silu_done"], j + 1)
                            dve.wait_ge(s["ups_full"], j + 1)
                            if pairs >= 1:
                                dve.wait_ge(s["hidden_hi"], j - 1)
                                dve.wait_ge(s["hidden_lo"], j - 1)
                            dve.tensor_tensor(fhd[:, c, :], fsg[:, pairs % 2, c, :], ps[:, b + 2 + c, :], ALU.mult)\
                               .then_inc(s["hidden"], 1)
                        for c in range(2):
                            j, chunk = 2 * pairs + c, 2 * p + c
                            dve.wait_ge(s["hidden_hi"], j + 1)
                            dve.tensor_tensor(fl[:, chunk, :], fhd[:, c, :], fh[:, chunk, :].bitcast(F32), ALU.subtract)\
                               .then_inc(s["hidden_lo"], 1)
                        pairs += 1
                    if half == 0:
                        for t in range(NT):
                            dve.wait_ge(s["products"], NT + t + 1)
                            y = res[:, t, :].rearrange("p (a b) -> p a b", a=2)
                            dve.scalar_tensor_tensor(y, y, ALPHA2, ps[:, 2 * t:2 * t + 2, :], ALU.mult, ALU.add)\
                               .then_inc(s["first_half_summed"], 1)
                barrier()
                layer_norm(1.0)
                assert links[0] == norm_links
            dve.wait_ge(s["normalised"], NT)
            residual_gain()
            dve.drain().then_inc(finished, 1)


_PLAIN = ["x", "w_in", "dt_bias", "a_log", "d_skip", "w_out", "ln1_g", "ln1_b",
          "w_gate", "w_up", "w_down", "ln2_g", "ln2_b", "mem_2", "w_in_2", "w_rg_2", 
          "w_ig_2", "w_br_rnn_2", "w_br_attn_2", "sinks_2", "w_out_2", "ln1_g_2", "ln1_b_2",
          "cq_w_2", "ckv_w_2", "co_w_2", "ln2_g_2", "ln2_b_2", "ffn_wi_2", "ffn_wo_2", "ln3_g_2", "ln3_b_2"]


_PER_FEATURE = ["conv_w", "conv_b", "ssd_norm_w", "ln1_g", "ln1_b", "ln2_g", "ln2_b", "conv_w_2", "conv_b_2", "b_rg_2",
                "b_ig_2", "lru_lambda_2", "ln1_g_2", "ln1_b_2", "ln2_g_2", "ln2_b_2", "ln3_g_2", "ln3_b_2"]


def kernel(**inputs):
    import concourse.bacc as bacc
    from concourse.bass_utils import run_bass_kernel_spmd

    data = {name: np.ascontiguousarray(inputs[name]) for name in _PLAIN}
    for name in _PER_FEATURE:
        a = inputs[name]
        a = np.moveaxis(np.asarray(a).reshape(*a.shape[:-1], -1, P), -1, 1)
        data[name + "_f"] = np.ascontiguousarray(a)
    data["w_route"] = np.concatenate([inputs["w_route_group"], inputs["w_route_expert"]], axis=-1)
    data["b_route"] = np.concatenate([inputs["b_route_group"], inputs["b_route_expert"]], axis=-1)
    data["tables"] = tables()
    nc = bacc.Bacc("TRN2", target_bir_lowering=False, num_devices=1)
    arrays, aps = {}, {}
    for name, a in data.items():
        arrays[f"in_{name}"] = a
        aps[name] = nc.dram_tensor(f"in_{name}", a.shape, mybir.dt.from_np(a.dtype), kind="ExternalInput").ap()
    out = nc.dram_tensor("out_0", (1, T, D), F32, kind="ExternalOutput").ap()
    build(nc, aps, out)
    r = run_bass_kernel_spmd(nc, [arrays], core_ids=[0])
    return r.results[0]["out_0"]
```
